# Optimizing a Trainium2 kernel written in Bass

```python
import math
import jax
import jax.numpy as jnp
from jax import lax
import numpy as np

D_MODEL = 1024
BATCH = 1
SEQ = 512
DEPTH = 2
DEC_BATCH = 8
DEC_SEQ = 4
PAST_LEN = 4096
PAGE_SIZE = 128

H_A = 4
DK_A = 32
DV_A = 64
GATE_RANK_A = 16
GATE_TAU_A = 16.0
H_B = 4
E_B = 64
DV_B = 64
H_C = 4
DK_C = 128
DV_C = 128
D_MIX = H_A * DV_A + H_B * DV_B + H_C * DV_C
D_FF = 2688
CHUNK = 64
EPS = 1e-6
M_INIT = -1e30
NEG_BIG = -1e30
SPLIT_SIZES = (
    H_A * DK_A, H_A * DK_A, H_A * DV_A, H_A * DV_A, GATE_RANK_A,
    H_B * E_B, H_B * E_B, H_B * DV_B, H_B * DV_B,
    H_C * DK_C, H_C * DK_C, H_C * DV_C, H_C * DV_C, H_C, H_C,
)
D_IN = sum(SPLIT_SIZES)

kernel_name = "hybrid_gla_hgrn2_mlstm_decoder_step"

def rmsnorm(x, g):
    xf = x.astype(jnp.float32)
    y = xf * lax.rsqrt(jnp.mean(xf * xf, axis=-1, keepdims=True) + EPS)
    return (y * g.astype(jnp.float32)).astype(x.dtype)

def swiglu(x, w_gate, w_up, w_down):
    return (jax.nn.silu(x @ w_gate) * (x @ w_up)) @ w_down

def to_chunks(x, c):
    b, t = x.shape[:2]
    return jnp.moveaxis(x.reshape((b, t // c, c) + x.shape[2:]), 1, 0)

def from_chunks(y):
    n, b, c = y.shape[:3]
    return jnp.moveaxis(y, 0, 1).reshape((b, n * c) + y.shape[3:])

def gated_linear_recurrence(q, k, v, log_a, s0):
    f32 = jnp.float32
    c = math.gcd(q.shape[1], CHUNK)
    causal = jnp.tril(jnp.ones((c, c), dtype=bool))[None, :, :, None, None]

    def step(s, inp):
        qc, kc, vc, gc = inp
        b = jnp.cumsum(gc, axis=1)
        rel = jnp.where(causal, b[:, :, None] - b[:, None, :], NEG_BIG)
        scores = jnp.einsum('bthk,bshk,btshk->bhts', qc, kc, jnp.exp(rel))
        o = (jnp.einsum('bhts,bshv->bthv', scores, vc)
             + jnp.einsum('bthk,bhkv->bthv', qc * jnp.exp(b), s))
        b_last = b[:, -1]
        s_new = (jnp.exp(b_last)[..., None] * s
                 + jnp.einsum('bshk,bshv->bhkv', kc * jnp.exp(b_last[:, None] - b), vc))
        return s_new, o

    xs = tuple(to_chunks(a.astype(f32), c) for a in (q, k, v, log_a))
    s_fin, o = lax.scan(step, s0.astype(f32), xs)
    return from_chunks(o), s_fin

def mlstm_recurrence(q, k, v, i_pre, f_pre, c0, n0, m0):
    f32 = jnp.float32
    c = math.gcd(q.shape[1], CHUNK)
    causal = jnp.tril(jnp.ones((c, c), dtype=bool))[None, :, :, None]

    def step(carry, inp):
        cm, n, m = carry
        qc, kc, vc, ic, fc = inp
        F = jnp.cumsum(jax.nn.log_sigmoid(fc), axis=1)
        log_d = jnp.where(causal, F[:, :, None] - F[:, None, :] + ic[:, None, :], NEG_BIG)
        log_prev = F + m[:, None]
        m_t = jnp.maximum(log_prev, jnp.max(log_d, axis=2))
        d = jnp.exp(log_d - m_t[:, :, None])
        w_prev = jnp.exp(log_prev - m_t)
        qk = jnp.einsum('bthk,bshk->btsh', qc, kc) * d
        num = (jnp.einsum('btsh,bshv->bthv', qk, vc)
               + w_prev[..., None] * jnp.einsum('bthk,bhkv->bthv', qc, cm))
        den = jnp.sum(qk, axis=2) + w_prev * jnp.einsum('bthk,bhk->bth', qc, n)
        h = num / jnp.maximum(jnp.abs(den), jnp.exp(-m_t))[..., None]
        m_new = m_t[:, -1]
        w_old = jnp.exp(F[:, -1] + m - m_new)
        w_s = jnp.exp(F[:, -1:] - F + ic - m_new[:, None])
        c_new = w_old[..., None, None] * cm + jnp.einsum('bsh,bshk,bshv->bhkv', w_s, kc, vc)
        n_new = w_old[..., None] * n + jnp.einsum('bsh,bshk->bhk', w_s, kc)
        return (c_new, n_new, m_new), h

    xs = tuple(to_chunks(a.astype(f32), c) for a in (q, k, v, i_pre, f_pre))
    carry0 = (c0.astype(f32), n0.astype(f32), m0.astype(f32))
    (c_fin, n_fin, m_fin), h = lax.scan(step, carry0, xs)
    return from_chunks(h), (c_fin, n_fin, m_fin)

def token_mixer(h, state, w_in, gla_w_lr, gla_b_lr, gla_norm, hgrn_lb, hgrn_norm,
                mlstm_i_bias, mlstm_f_bias, mlstm_norm, w_out):
    bsz, t, _ = h.shape
    f32 = jnp.float32
    split_at = np.cumsum(SPLIT_SIZES)[:-1].tolist()
    (a_q, a_k, a_v, a_g, a_lr, b_q, b_f, b_i, b_g,
     c_q, c_k, c_v, c_o, c_i, c_f) = jnp.split(h @ w_in, split_at, axis=-1)
    heads = lambda u, n: u.reshape(bsz, t, n, -1)
    s_gla, s_hgrn, c_mem, n_vec, m_vec = state

    log_alpha = jax.nn.log_sigmoid((a_lr @ gla_w_lr + gla_b_lr).astype(f32)) / GATE_TAU_A
    o_a, s_gla_new = gated_linear_recurrence(
        heads(a_q, H_A) * DK_A ** -0.5, heads(a_k, H_A), heads(a_v, H_A), heads(log_alpha, H_A), s_gla)
    o_a = rmsnorm(o_a, gla_norm) * jax.nn.silu(heads(a_g, H_A).astype(f32))

    lb = hgrn_lb.reshape(H_B, E_B)
    z = heads(b_f, H_B).astype(f32)
    k_b = (1.0 - lb) * jax.nn.sigmoid(-z)
    log_f = jnp.log1p(-k_b)
    o_b, s_hgrn_new = gated_linear_recurrence(
        jax.nn.silu(heads(b_q, H_B)), k_b, heads(b_i, H_B), log_f, s_hgrn)
    o_b = rmsnorm(o_b, hgrn_norm) * jax.nn.silu(heads(b_g, H_B).astype(f32))

    h_c, (c_new, n_new, m_new) = mlstm_recurrence(
        heads(c_q, H_C), heads(c_k, H_C) * DK_C ** -0.5, heads(c_v, H_C),
        c_i + mlstm_i_bias, c_f + mlstm_f_bias, c_mem, n_vec, m_vec)
    o_c = jax.nn.sigmoid(heads(c_o, H_C).astype(f32)) * rmsnorm(h_c, mlstm_norm)

    mixed = jnp.concatenate(
        [o_a.reshape(bsz, t, -1), o_b.reshape(bsz, t, -1), o_c.reshape(bsz, t, -1)], axis=-1).astype(h.dtype)
    return mixed @ w_out, (s_gla_new, s_hgrn_new, c_new, n_new, m_new)

def decoder_layer(x, state, norm_gains, ffn1_w_gate, ffn1_w_up, ffn1_w_down, w_in, gla_w_lr, gla_b_lr,
                  gla_norm, hgrn_lb, hgrn_norm, mlstm_i_bias, mlstm_f_bias, mlstm_norm, w_out,
                  ffn2_w_gate, ffn2_w_up, ffn2_w_down):
    g = norm_gains
    x = x + 0.5 * rmsnorm(swiglu(rmsnorm(x, g[0]), ffn1_w_gate, ffn1_w_up, ffn1_w_down), g[1])
    mix, new_state = token_mixer(rmsnorm(x, g[2]), state, w_in, gla_w_lr, gla_b_lr, gla_norm, hgrn_lb,
                                 hgrn_norm, mlstm_i_bias, mlstm_f_bias, mlstm_norm, w_out)
    x = x + rmsnorm(mix, g[3])
    x = x + 0.5 * rmsnorm(swiglu(rmsnorm(x, g[4]), ffn2_w_gate, ffn2_w_up, ffn2_w_down), g[5])
    return x, new_state

def setup_inputs(seed: int = 0) -> dict:
    key = jax.random.key(seed)
    ks = jax.random.split(key, 24)
    f32 = jnp.float32
    nrm = lambda k, shape, scale: scale * jax.random.normal(k, shape, f32)
    return {
        'x_prompt': nrm(ks[0], (BATCH, SEQ, D_MODEL), 1.0),
        'x_sample': nrm(ks[1], (DEC_BATCH, DEC_SEQ, D_MODEL), 1.0),
        'state_gla': nrm(ks[2], (DEPTH, DEC_BATCH, H_A, DK_A, DV_A), 1.0),
        'state_hgrn': nrm(ks[3], (DEPTH, DEC_BATCH, H_B, E_B, DV_B), 1.0),
        'state_mlstm_C': nrm(ks[4], (DEPTH, DEC_BATCH, H_C, DK_C, DV_C), 0.5),
        'state_mlstm_n': nrm(ks[5], (DEPTH, DEC_BATCH, H_C, DK_C), 0.5),
        'state_mlstm_m': 1.0 + nrm(ks[6], (DEPTH, DEC_BATCH, H_C), 0.5),
        'norm_gains': 1.0 + nrm(ks[7], (DEPTH, 6, D_MODEL), 0.05),
        'ffn1_w_gate': nrm(ks[8], (DEPTH, D_MODEL, D_FF), D_MODEL ** -0.5),
        'ffn1_w_up': nrm(ks[9], (DEPTH, D_MODEL, D_FF), D_MODEL ** -0.5),
        'ffn1_w_down': nrm(ks[10], (DEPTH, D_FF, D_MODEL), D_FF ** -0.5),
        'w_in': nrm(ks[11], (DEPTH, D_MODEL, D_IN), D_MODEL ** -0.5),
        'gla_w_lr': nrm(ks[12], (DEPTH, GATE_RANK_A, H_A * DK_A), GATE_RANK_A ** -0.5),
        'gla_b_lr': nrm(ks[13], (DEPTH, H_A * DK_A), 0.1),
        'gla_norm': 1.0 + nrm(ks[14], (DEPTH, DV_A), 0.05),
        'hgrn_lb_logits': nrm(ks[15], (DEPTH, H_B * E_B), 1.0),
        'hgrn_norm': 1.0 + nrm(ks[16], (DEPTH, DV_B), 0.05),
        'mlstm_i_bias': nrm(ks[17], (DEPTH, H_C), 0.1),
        'mlstm_f_bias': jnp.linspace(3.0, 6.0, H_C, dtype=f32)[None, :] + nrm(ks[18], (DEPTH, H_C), 0.1),
        'mlstm_norm': 1.0 + nrm(ks[19], (DEPTH, DV_C), 0.05),
        'w_out': nrm(ks[20], (DEPTH, D_MIX, D_MODEL), D_MIX ** -0.5),
        'ffn2_w_gate': nrm(ks[21], (DEPTH, D_MODEL, D_FF), D_MODEL ** -0.5),
        'ffn2_w_up': nrm(ks[22], (DEPTH, D_MODEL, D_FF), D_MODEL ** -0.5),
        'ffn2_w_down': nrm(ks[23], (DEPTH, D_FF, D_MODEL), D_FF ** -0.5),
    }

def reference(x_prompt, x_sample, state_gla, state_hgrn, state_mlstm_C, state_mlstm_n, state_mlstm_m,
              norm_gains, ffn1_w_gate, ffn1_w_up, ffn1_w_down, w_in, gla_w_lr, gla_b_lr, gla_norm,
              hgrn_lb_logits, hgrn_norm, mlstm_i_bias, mlstm_f_bias, mlstm_norm, w_out,
              ffn2_w_gate, ffn2_w_up, ffn2_w_down):
    f32 = jnp.float32
    lb_sm = jax.nn.softmax(hgrn_lb_logits.astype(f32), axis=0)
    lb_all = jnp.cumsum(lb_sm, axis=0) - lb_sm[0:1]
    zero_state = (
        jnp.zeros((BATCH, H_A, DK_A, DV_A), f32),
        jnp.zeros((BATCH, H_B, E_B, DV_B), f32),
        jnp.zeros((BATCH, H_C, DK_C, DV_C), f32),
        jnp.zeros((BATCH, H_C, DK_C), f32),
        jnp.full((BATCH, H_C), M_INIT, f32),
    )
    y_prompt, y_sample = x_prompt, x_sample
    prompt_states, sample_states = [], []
    for l in range(DEPTH):
        weights = (norm_gains[l], ffn1_w_gate[l], ffn1_w_up[l], ffn1_w_down[l], w_in[l], gla_w_lr[l],
                   gla_b_lr[l], gla_norm[l], lb_all[l], hgrn_norm[l], mlstm_i_bias[l], mlstm_f_bias[l],
                   mlstm_norm[l], w_out[l], ffn2_w_gate[l], ffn2_w_up[l], ffn2_w_down[l])
        y_prompt, st_p = decoder_layer(y_prompt, zero_state, *weights)
        past = (state_gla[l], state_hgrn[l], state_mlstm_C[l], state_mlstm_n[l], state_mlstm_m[l])
        y_sample, st_s = decoder_layer(y_sample, past, *weights)
        prompt_states.append(st_p)
        sample_states.append(st_s)
    gla_p, hgrn_p, c_p, n_p, m_p = (jnp.stack(s) for s in zip(*prompt_states))
    gla_s, hgrn_s, c_s, n_s, m_s = (jnp.stack(s) for s in zip(*sample_states))
    return (y_prompt, y_sample, gla_p, hgrn_p, c_p, n_p, m_p, gla_s, hgrn_s, c_s, n_s, m_s)


_drawn_inputs = setup_inputs


def setup_inputs(seed=0):
    import zlib

    import numpy as np

    out = dict(_drawn_inputs(seed))
    spreads = {}
    factors = {}
    for name, (base, spread) in spreads.items():
        noise = np.random.default_rng([zlib.crc32(name.encode()), seed]).standard_normal(out[name].shape)
        drawn = base * np.exp(spread * noise) if base else spread * noise
        out[name] = jnp.asarray(drawn.astype(out[name].dtype))
    for name, factor in factors.items():
        out[name] = (out[name] * factor).astype(out[name].dtype)
    return out
```

```python
from contextlib import ExitStack

import numpy as np

import concourse.bass as bass
from concourse import mybir

F32 = mybir.dt.float32
F32R = mybir.dt.float32r
U8 = mybir.dt.uint8
ALU = mybir.AluOpType
ACT = mybir.ActivationFunctionType

P = 128
NEG = -1e30


def program(nc, I, O):
    DEPTH, D, FF = I["ffn1_w_gate"].shape
    SEQ = I["x_prompt"].shape[1]
    NB, DS, _ = I["x_sample"].shape
    HA, DKA, DVA = I["state_gla"].shape[2:]
    HB, DKB, DVB = I["state_hgrn"].shape[2:]
    HC, DKC, DVC = I["state_mlstm_C"].shape[2:]
    RANK = I["gla_w_lr"].shape[1]
    NS = NB * DS
    T = SEQ + NS
    HT = T // 2
    DC = D // P
    FC = FF // P
    NCH = SEQ // P
    EPS = 1e-6
    TAU = 16.0
    assert D == 8 * P and FF % P == 0 and T == 544 and DKC == DVC == P and HA * DKA == P

    AQ, AK, AV, AG = 0, 1, 2, 4
    BQ, BF, BI, BG = 6, 8, 10, 12
    CQ, CK, CV, CO = 14, 18, 22, 26
    NPROJ = 30
    LR_COL = AG * P + HA * DVA
    IF_COL = NPROJ * P + RANK

    RING, RAW, LEAD = 6, 3, 4
    DOWN_BLOCKS = -(-FC // 4)
    B_UP1 = 0
    B_DN1 = B_UP1 + 4 * FC
    B_IN = B_DN1 + DOWN_BLOCKS * DC
    B_OUT = B_IN + 2 * NPROJ
    B_UP2 = B_OUT + 2 * DC
    B_DN2 = B_UP2 + 4 * FC

    GATED = 15
    assert GATED >= CQ and GATED % 3 == 0

    def down_size(q):
        return FC - 4 * (DOWN_BLOCKS - 1) if q % DOWN_BLOCKS == DOWN_BLOCKS - 1 else 4

    def four(q):
        return 4

    LEVELS = [1, 2, 4, 8, 16, 32, 64]
    NL = len(LEVELS)
    SCORE = [("diag", 0)] + [("level", r) for r in range(NL)] + [("samples", 0)]
    SAMPLE_LEVELS = [r for r, h in enumerate(LEVELS) if 2 * h <= DS]
    LIN = len(SCORE) + 5
    NCT = 3
    SEQUENCE = [("spread", 0), ("norm", 0), ("qk", 0), ("norm", 1), ("own", 0)]
    for h in range(HC):
        if h:
            SEQUENCE += [("qk", h), ("own", h), ("samples", h - 1)]
        SEQUENCE += [("spread", h + 1) if h + 1 < HC else ("norm", 2), ("out", h)]
    SEQUENCE += [("samples", HC - 1), ("norm", 3)]
    NROUND = NCT * LIN + len(SEQUENCE)

    def place(kind, n):
        return NCT * LIN + SEQUENCE.index((kind, n))

    with ExitStack() as ctx:
        top = [16512]
        NPAR = 6 * DC + 1 + 3

        def at(name, shape, dtype, offset):
            return nc.alloc_sbuf_tensor_at(name, shape, dtype, offset=offset)

        def nbytes(shape, dtype):
            n = int(np.prod(shape[1:])) * (1 if dtype == U8 else 4)
            return (n + 31) // 32 * 32

        def new(name, shape, dtype=F32):
            off = top[0]
            top[0] += nbytes(shape, dtype)
            return at(name, shape, dtype, off)

        def sub(cursor, name, shape, dtype=F32):
            off = cursor[0]
            cursor[0] += nbytes(shape, dtype)
            assert cursor[0] <= cursor[1], name
            return at(name, shape, dtype, off)

        x = new("x", [P, DC, T])
        xn_at = top[0]
        xn_hi = new("xn_hi", [P, DC, T], F32R)
        xn_lo = new("xn_lo", [P, DC, T], F32R)
        xn_end = top[0]
        y_ffn = at("y_ffn", [P, DC, T], F32, xn_at)
        h_at = top[0]
        h_hi = new("h_hi", [P, FC, T], F32R)
        h_lo = new("h_lo", [P, FC, T], F32R)
        h_end = top[0]
        w_hi = new("w_hi", [P, RING, 4 * P], F32R)
        w_lo = new("w_lo", [P, RING, 4 * P], F32R)
        w_raw = new("w_raw", [P, RAW, 4 * P])
        tmp_at = top[0]
        gs = new("gs", [P, 3, T])
        acc = new("acc", [P, T])
        std = new("std", [P, T])
        rstd = new("rstd", [P, T])
        tmp_end = top[0]

        c1 = [h_at, h_end]
        proj = sub(c1, "proj", [P, NPROJ, T])
        qk_l = sub(c1, "qk_l", [P, 2, 2, T])
        ex_l = sub(c1, "ex_l", [P, 2, T])
        q_st = sub(c1, "q_st", [P, T])
        k_st = sub(c1, "k_st", [P, T])
        e_st = sub(c1, "e_st", [P, T])
        bcum = sub(c1, "bcum", [P, NCT, T])
        small_raw = at("small_raw", [P, DC, 68], F32, c1[1] - nbytes([P, NCT, T], F32))
        c4 = [h_at + nbytes([P, NPROJ, T], F32), h_end]
        head_std = sub(c4, "head_std", [P, 4, T])
        head_sq = sub(c4, "head_sq", [P, 3, T])
        mix2 = [sub(c4, name, [P, T]) for name in ("dmat2", "wprev2", "enm2")]
        s_c2 = sub(c4, "s_c2", [P, NB, DVC])
        y_mix = at("y_mix", [P, DC, T], F32, h_at)
        x_sq = at("x_sq", [P, DC, T], F32, h_at + nbytes([P, DC, T], F32))
        tok_in = at("tok_in", [P, NCH + 1, D], F32, h_at)
        par_raw = at("par_raw", [DEPTH * NPAR, P], F32, h_at + nbytes([P, NCH + 1, D], F32))
        tok_out = at("tok_out", [P, NCH + 1, D], F32, h_at)
        c2 = [xn_at, xn_end]
        scores = sub(c2, "scores", [P, 4, NCH * P])
        scores_s = sub(c2, "scores_s", [NS, 4, NS])
        v_tok = sub(c2, "v_tok", [P, 2, NCH * P])
        v_tok_s = sub(c2, "v_tok_s", [NS, 2, P])
        k_tok = sub(c2, "k_tok", [P, NCH * P])
        k_tok_s = sub(c2, "k_tok_s", [NS, 2, P])
        v_exp = sub(c2, "v_exp", [NS, NB * P])
        mix1 = [sub(c2, name, [P, T]) for name in ("dmat1", "wprev1", "enm1")]
        dmats, wprevs, enms = zip(mix1, mix2)
        c_st = sub(c2, "c_st", [P, NCH, P])
        lin_st = sub(c2, "lin_st", [P, NCT, NCH, DVA])
        pmat = scores
        c3 = [tmp_at, tmp_end]
        row_g = sub(c3, "row_g", [HC, T])
        row_f = sub(c3, "row_f", [HC, T])
        row_m = sub(c3, "row_m", [HC, T])
        row_a = sub(c3, "row_a", [HC, T])
        row_mt = sub(c3, "row_mt", [HC, T])
        row_w = row_f
        SPREAD_ROWS = (row_m, row_a, row_mt)
        row_at = {name: tmp_at + i * nbytes([HC, T], F32) for i, name in enumerate("gfmatr")}
        ROW_PARTS = [(at("hi_" + hi, [HC, T], F32R, row_at[hi]), at("lo_" + lo, [HC, T], F32R, row_at[lo]))
                     for hi, lo in (("f", "m"), ("g", "a"), ("r", "t"))]

        s_lin = new("s_lin", [P, NCT, NB, DVA])
        s_cs = [new("s_c1", [P, NB, DVC]), s_c2]
        ident = new("ident", [P, P])
        ones = new("ones", [P, P])
        blk = new("blk", [P, P])
        causal = new("causal", [P, P])
        causal_s = new("causal_s", [NS, NS])
        bmask = new("bmask", [NS, NB])
        sel = new("sel", [HC, HC, P])
        lmask = new("lmask", [P, NL, P], U8)
        neg_s = new("neg_s", [HC, NS])
        reset = new("reset", [P, T])
        sel_r = at("sel_r", [HC, HC, P], F32R, top[0])
        small_hi = new("small_hi", [P, DC, 68], F32R)
        small_lo = new("small_lo", [P, DC, 68], F32R)
        par_all = new("par_all", [P, DEPTH, NPAR])
        par = new("par", [P, NPAR])
        nrow = new("nrow", [NS + HC, P])
        n_s = new("n_s", [P, NS])
        n_all = new("n_all", [P, NS + HC])
        n_ch = new("n_ch", [P, NCH])
        lb_raw = new("lb_raw", [2 * DEPTH, P])
        lbw = new("lbw", [P, 4])
        lb_e = new("lb_e", [P, DEPTH, 2])
        omlb = new("omlb", [P, DEPTH, 2])
        omlb_l = new("omlb_l", [P, 2])
        wlr = new("wlr", [RANK, P])
        eps_t = new("eps_t", [P, 1])
        bias_if = new("bias_if", [HC, 2])
        m_s = new("m_s", [HC, NB])
        m_new = new("m_new", [HC, NB])
        m_ch = new("m_ch", [HC, NCH + 1])
        g_s = new("g_s", [HC, NS])
        gcol = new("gcol", [P, (NCH + 1) * HC])
        wcol = new("wcol", [P, (NCH + 1) * HC])
        assert top[0] <= 229368
        ps = ctx.enter_context(nc.psum_tensor("ps", [P, 8, 512], F32))

        BLR_ROW, GN_ROW = 6 * DC, 6 * DC + 1

        sems = []

        def sem(name):
            s = ctx.enter_context(nc.semaphore(name))
            sems.append(s)
            return s

        const_ready = sem("const_ready")
        lb_loaded = sem("lb_loaded")
        lb_mm = sem("lb_mm")
        lb_step = sem("lb_step")
        tok_loaded = sem("tok_loaded")
        tok_turned = sem("tok_turned")
        par_arrived = sem("par_arrived")
        par_turned = sem("par_turned")
        tok_kept = sem("tok_kept")
        out_turned = sem("out_turned")
        out_kept = sem("out_kept")
        out_stored = sem("out_stored")
        first = len(sems)
        w_arrived = [sem(f"w_arrived{i}") for i in range(RAW)]
        w_hi_ready = sem("w_hi_ready")
        w_split = sem("w_split")
        w_used = sem("w_used")
        small_arrived = sem("small_arrived")
        small_zero = sem("small_zero")
        small_hi_ready = sem("small_hi_ready")
        small_split = sem("small_split")
        par_kept = sem("par_kept")
        silu_done = sem("silu_done")
        gate_scaled = sem("gate_scaled")
        up_read = sem("up_read")
        h_scaled = sem("h_scaled")
        h_hi_ready = sem("h_hi_ready")
        h_ready = sem("h_ready")
        y_copied = sem("y_copied")
        y_squared = sem("y_squared")
        y_summed = sem("y_summed")
        acc_zero = sem("acc_zero")
        x_squared = sem("x_squared")
        x_summed = sem("x_summed")
        xsq_done = sem("xsq_done")
        ssq_done = sem("ssq_done")
        std_done = sem("std_done")
        rstd_done = sem("rstd_done")
        y_scaled = sem("y_scaled")
        x_updated = sem("x_updated")
        xn_hi_ready = sem("xn_hi_ready")
        xn_ready = sem("xn_ready")
        proj_read = sem("proj_read")
        small_done = sem("small_done")
        rows_read = sem("rows_read")
        lowrank_done = sem("lowrank_done")
        u_ready = sem("u_ready")
        lsig_step = sem("lsig_step")
        gates_done = sem("gates_done")
        omlb_ready = sem("omlb_ready")
        kb_ready = sem("kb_ready")
        logf_ready = sem("logf_ready")
        cum_ready = sem("cum_ready")
        row_step = sem("row_step")
        cols_turned = sem("cols_turned")
        cols_kept = sem("cols_kept")
        wcol_ready = sem("wcol_ready")
        rows_high = sem("rows_high")
        rows_split = sem("rows_split")
        expo_arg = sem("expo_arg")
        expo_val = sem("expo_val")
        qk_ready = sem("qk_ready")
        scaled = sem("scaled")
        st_arg = sem("st_arg")
        st_val = sem("st_val")
        st_scaled = sem("st_scaled")
        round_done = sem("round_done")
        round_read = sem("round_read")
        vexp_ready = sem("vexp_ready")
        vexp_used = sem("vexp_used")
        st_step = sem("st_step")
        slin_arrived = sem("slin_arrived")
        sc_arrived = [sem("sc_arrived0"), sem("sc_arrived1")]
        n_arrived = sem("n_arrived")
        n_turned = sem("n_turned")
        n_kept = sem("n_kept")
        ms_arrived = sem("ms_arrived")
        c_val = sem("c_val")
        d_ready = sem("d_ready")
        tok_ready = sem("tok_ready")
        c_step = sem("c_step")
        cp_stored = sem("cp_stored")
        cs_stored = sem("cs_stored")
        den_abs = sem("den_abs")
        n_out_turned = sem("n_out_turned")
        n_out_kept = sem("n_out_kept")
        state_stored = sem("state_stored")
        o_squared = sem("o_squared")
        o_ssq = sem("o_ssq")
        o_std = sem("o_std")
        o_norm = sem("o_norm")
        o_ln = sem("o_ln")
        o_gated = sem("o_gated")
        m_hi_ready = sem("m_hi_ready")
        m_ready = sem("m_ready")
        loop_sems = sems[first:]

        def pair(p):
            return ps[:, 2 * p:2 * p + 2, 0:HT]

        def halves(ap):
            return ap.rearrange("p (a n) -> p a n", a=2)

        def tiles(eng, total, body, emit, head=0, peel=0):
            full = (total - peel) // body
            if full - head < 2:
                head = full
            for t in range(head * body):
                emit(t, t % body, t // body)
            if full > head:
                with eng.Fori(head, full) as i:
                    for j in range(body):
                        emit(i * body + j, j, i)
            for t in range(full * body, total):
                emit(t, t % body, t // body)

        def proj_groups():
            return [(0, BQ, 0), (BQ, NPROJ - BQ, RANK)]

        def raw_view(ap, n):
            return ap.rearrange("p (c n) -> p c n", n=P)[:, 0:n, :]

        ident_step = []
        with nc.Block() as block:

            @block.gpsimd
            def _(pool):
                n = [0]

                def make(ins):
                    n[0] += 1
                    ins.then_inc(const_ready, 1)
                    pool.wait_ge(const_ready, n[0])

                make(pool.memset(ident[:], 0.0))
                make(pool.affine_select(out=ident[:], in_=ident[:], compare_op=ALU.not_equal, fill=1.0, base=0,
                                   pattern=[[-1, P]], channel_multiplier=1))
                n_ident = n[0]
                make(pool.memset(eps_t[:], EPS))
                make(pool.memset(ones[:], 1.0))
                make(pool.memset(blk[:], 0.0))
                make(pool.memset(causal[:], 0.0))
                make(pool.memset(causal_s[:], 0.0))
                make(pool.memset(bmask[:], 1.0))
                make(pool.memset(sel[:], 0.0))
                make(pool.memset(neg_s[:], 0.0))
                make(pool.memset(reset[:], 1.0))
                make(pool.memset(gs[:], 0.0))
                for r, h in enumerate(LEVELS):
                    m = gs[:, 0, 0:P].rearrange("p (b n) -> p b n", n=2 * h)
                    if r:
                        make(pool.memset(gs[:, 0, 0:P], 0.0))
                    make(pool.memset(m[:, :, h:2 * h], 1.0))
                    make(pool.affine_select(out=m[:, :, h:2 * h], in_=m[:, :, h:2 * h], compare_op=ALU.is_ge, fill=0.0,
                                       base=0, pattern=[[-2 * h, P // (2 * h)], [0, h]],
                                       channel_multiplier=1))
                    make(pool.affine_select(out=m[:, :, h:2 * h], in_=m[:, :, h:2 * h], compare_op=ALU.is_ge, fill=0.0,
                                       base=h - 1, pattern=[[2 * h, P // (2 * h)], [0, h]],
                                       channel_multiplier=-1))
                    make(pool.tensor_copy(lmask[:, r, :], gs[:, 0, 0:P]))
                for half in range(2):
                    make(pool.memset(blk[64 * half:64 * half + 64, 64 * half:64 * half + 64], 1.0))
                make(pool.affine_select(out=causal[:], in_=causal[:], compare_op=ALU.is_ge, fill=NEG, base=0,
                                   pattern=[[1, P]], channel_multiplier=-1))
                make(pool.affine_select(out=causal_s[:], in_=causal_s[:], compare_op=ALU.is_ge, fill=NEG, base=0,
                                   pattern=[[1, NS]], channel_multiplier=-1))
                make(pool.affine_select(out=bmask[:], in_=bmask[:], compare_op=ALU.is_ge, fill=0.0, base=0,
                                   pattern=[[-DS, NB]], channel_multiplier=1))
                make(pool.affine_select(out=sel[:], in_=sel[:], compare_op=ALU.not_equal, fill=1.0, base=0,
                                   pattern=[[-1, HC], [0, P]], channel_multiplier=1))
                make(pool.memset(neg_s[:].rearrange("p (b n) -> p b n", n=DS)[:, :, 0:1], -3e38))
                make(pool.memset(reset[:, 0:SEQ].rearrange("p (b n) -> p b n", n=P)[:, :, 0:1], 0.0))
                make(pool.memset(reset[:, SEQ:T].rearrange("p (b n) -> p b n", n=DS)[:, :, 0:1], 0.0))
                cs = causal_s[:].rearrange("p (b n) -> p b n", n=DS)
                make(pool.affine_select(out=cs, in_=cs, compare_op=ALU.is_ge, fill=NEG, base=0,
                                   pattern=[[-DS, NB], [0, DS]], channel_multiplier=1))
                make(pool.affine_select(out=bmask[:], in_=bmask[:], compare_op=ALU.is_ge, fill=0.0, base=DS - 1,
                                   pattern=[[DS, NB]], channel_multiplier=-1))
                ident_step.append(n_ident)

            @block.sync
            def _(sp):
                sp.dma_start(tok_in[:, 0:NCH, :], I["x_prompt"].rearrange("a (c p) d -> p (a c) d", p=P)
                             ).then_inc(tok_loaded, 16)
                sp.dma_start(tok_in[0:NS, NCH, :], I["x_sample"].rearrange("b t d -> (b t) d")).then_inc(tok_loaded, 16)
                for l in range(DEPTH):
                    sp.dma_start(lb_raw[2 * l:2 * l + 2, :],
                                 I["hgrn_lb_logits"][l].rearrange("(c p) -> c p", p=P)).then_inc(lb_loaded, 16)
                    r0 = l * NPAR
                    sp.dma_start(par_raw[r0:r0 + 6 * DC, :], I["norm_gains"][l].rearrange("g (c p) -> (g c) p", p=P)
                                 ).then_inc(par_arrived, 16)
                    sp.dma_start(par_raw[r0 + BLR_ROW:r0 + BLR_ROW + 1, :], I["gla_b_lr"][l:l + 1, :]).then_inc(par_arrived, 16)
                    for half in range(2):
                        hs = slice(64 * half, 64 * half + 64)
                        sp.dma_start(par_raw[r0 + GN_ROW:r0 + GN_ROW + 1, hs], I["gla_norm"][l:l + 1, :]).then_inc(par_arrived, 16)
                        sp.dma_start(par_raw[r0 + GN_ROW + 1:r0 + GN_ROW + 2, hs], I["hgrn_norm"][l:l + 1, :]
                                     ).then_inc(par_arrived, 16)
                    sp.dma_start(par_raw[r0 + GN_ROW + 2:r0 + GN_ROW + 3, :], I["mlstm_norm"][l:l + 1, :]).then_inc(par_arrived, 16)

            @block.tensor
            def _(pe):
                pe.wait_ge(const_ready, ident_step[0])
                pe.wait_ge(tok_loaded, 32)
                for c in range(DC):
                    if c >= 4:
                        pe.wait_ge(tok_kept, c - 3)
                    b = 2 * (c % 4)
                    for j in range(NCH):
                        pe.transpose(ps[:, b, j * P:j * P + P], tok_in[:, j, c * P:c * P + P], ident[:])
                    pe.transpose(ps[:, b + 1, 0:NS], tok_in[0:NS, NCH, c * P:c * P + P],
                                 ident[0:NS, 0:NS]).then_inc(tok_turned, 1)
                pe.wait_ge(lb_loaded, 32)
                pe.wait_ge(tok_kept, DC)
                pe.transpose(ps[:, 0, 0:2 * DEPTH], lb_raw[:], ident[0:2 * DEPTH, 0:2 * DEPTH]).then_inc(lb_mm, 1)
                pe.wait_ge(par_arrived, 16 * 7 * DEPTH)
                pe.transpose(ps[:, 2, 0:DEPTH * NPAR], par_raw[:], ident[0:DEPTH * NPAR, 0:DEPTH * NPAR]).then_inc(par_turned, 1)

            @block.vector
            def _(dve):
                for c in range(DC):
                    dve.wait_ge(tok_turned, c + 1)
                    b = 2 * (c % 4)
                    dve.tensor_copy(x[:, c, 0:SEQ], ps[:, b, 0:SEQ])
                    dve.tensor_copy(x[:, c, SEQ:T], ps[:, b + 1, 0:NS]).then_inc(tok_kept, 1)
                n = [0]

                def step(ins):
                    n[0] += 1
                    ins.then_inc(lb_step, 1)
                    dve.wait_ge(lb_step, n[0])

                logit = [ps[:, 0, 2 * l:2 * l + 2] for l in range(DEPTH)]
                mx, tot = lbw[:, 0:2], lbw[:, 2:4]
                dve.wait_ge(lb_mm, 1)
                step(dve.tensor_copy(mx, logit[0]))
                for l in range(1, DEPTH):
                    step(dve.tensor_tensor(mx, logit[l], mx, ALU.max))
                for l in range(DEPTH):
                    step(dve.tensor_tensor(lb_e[:, l, :], logit[l], mx, ALU.subtract))
                n[0] += DEPTH
                dve.wait_ge(lb_step, n[0])
                step(dve.tensor_copy(tot, lb_e[:, 0, :]))
                for l in range(1, DEPTH):
                    step(dve.tensor_tensor(tot, tot, lb_e[:, l, :], ALU.add))
                step(dve.reciprocal(tot, tot))
                for l in range(DEPTH):
                    step(dve.tensor_tensor(lb_e[:, l, :], lb_e[:, l, :], tot, ALU.mult))
                step(dve.tensor_copy(mx, lb_e[:, 0, :]))
                for l in range(DEPTH):
                    if l:
                        step(dve.tensor_tensor(mx, mx, lb_e[:, l, :], ALU.add))
                    step(dve.tensor_tensor(omlb[:, l, :], mx, lb_e[:, 0, :], ALU.subtract))
                    step(dve.tensor_scalar(omlb[:, l, :], omlb[:, l, :], -1.0, 1.0, ALU.mult, ALU.add))
                dve.wait_ge(par_turned, 1)
                step(dve.tensor_copy(par_all[:].rearrange("p l n -> p (l n)"), ps[:, 2, 0:DEPTH * NPAR]))
                for l in range(DEPTH):
                    for g in (1, 5):
                        dve.tensor_scalar(par_all[:, l, g * DC:g * DC + DC], par_all[:, l, g * DC:g * DC + DC], 0.5, None, ALU.mult)

            @block.scalar
            def _(act):
                act.wait_ge(lb_step, 2 * DEPTH)
                for l in range(DEPTH):
                    act.activation(lb_e[:, l, :], lb_e[:, l, :], ACT.Exp).then_inc(lb_step, 1)

        KS = float(DKC) ** -0.5
        O_TILES = [AV, AV + 1, BI, BI + 1, CV, CV + 1, CV + 2, CV + 3]
        GATE_TILES = [AG, AG + 1, BG, BG + 1, CO, CO + 1, CO + 2, CO + 3]

        def q_tile(ct):
            return AQ if ct == 0 else BQ + ct - 1

        def k_tile(ct):
            return AK if ct == 0 else BF + ct - 1

        def v_tiles(ct):
            return [AV, AV + 1] if ct == 0 else [BI + ct - 1]

        def heads(ct):
            dk = DKA if ct == 0 else DKB
            return [(hh, slice(dk * hh, dk * hh + dk), hh // 2, 64 * (hh % 2)) for hh in range(P // dk)]

        ROW_STEPS = 16 + 2 * NCH

        def layer(l, block):

            @block.sync
            def _(sp):
                def load(n, q, size, src):
                    sp.wait_ge(w_split, n + 1)
                    sp.dma_start(raw_view(w_raw[:, q % RAW, :], size(q)), src).then_inc(w_arrived[q % RAW], 16)

                def rows(w, k0, k1, col):
                    return w[bass.ds(l, 1), k0 * P:k1 * P, bass.ds(col, P)].rearrange("a (c p) n -> p (a c) n", p=P)

                def load_up(base, gate, up):
                    def emit(t, j, i):
                        for b, w in enumerate((gate, gate, up, up)):
                            k = 4 * (b % 2)
                            load(base + t * 4 + b, base + 4 * j + b, four, rows(w, k, k + 4, t * P))
                    tiles(sp, FC, 3, emit)

                def load_down(base, w):
                    def emit(t, j, i):
                        for b in range(DOWN_BLOCKS):
                            load(base + t * DOWN_BLOCKS + b, base + DOWN_BLOCKS * j + b,
                                 lambda q: min(4, FC - 4 * b), rows(w, 4 * b, min(4 * b + 4, FC), t * P))
                    tiles(sp, DC, 2, emit)

                load_up(B_UP1, I["ffn1_w_gate"], I["ffn1_w_up"])
                sp.dma_start(nrow[0:NS, :], I["state_mlstm_n"][bass.ds(l, 1)].rearrange("a b h k -> (a b h) k")
                             ).then_inc(n_arrived, 16)
                sp.dma_start(wlr[:], I["gla_w_lr"][bass.ds(l, 1)].rearrange("a r n -> (a r) n")).then_inc(small_arrived, 16)
                sp.dma_start(bias_if[:, 0:1], I["mlstm_i_bias"][bass.ds(l, 1), :].rearrange("a h -> h a")).then_inc(small_arrived, 16)
                sp.dma_start(bias_if[:, 1:2], I["mlstm_f_bias"][bass.ds(l, 1), :].rearrange("a h -> h a")).then_inc(small_arrived, 16)
                sp.dma_start(m_s[:], I["state_mlstm_m"][bass.ds(l, 1)].rearrange("a b h -> h (a b)"),
                             allow_slow_non_contiguous=True).then_inc(ms_arrived, 16)
                sp.dma_start(s_lin[:, 0], I["state_gla"][bass.ds(l, 1)].rearrange("a b h k v -> (h k) (a b) v")).then_inc(slin_arrived, 16)
                for j in range(2):
                    sp.dma_start(s_lin[:, 1 + j], I["state_hgrn"][bass.ds(l, 1), :, 2 * j:2 * j + 2].rearrange(
                        "a b h k v -> (h k) (a b) v")).then_inc(slin_arrived, 16)
                load_down(B_DN1, I["ffn1_w_down"])

                def load_in(t0, count, shift):
                    def emit(t, j, i):
                        for b in range(2):
                            load(B_IN + (t0 + t) * 2 + b, B_IN + 2 * j + b, four,
                                 rows(I["w_in"], 4 * b, 4 * b + 4, (t0 + t) * P + shift))
                    tiles(sp, count, 3, emit)
                for t0, count, shift in proj_groups():
                    load_in(t0, count, shift)
                    if shift:
                        continue
                    sp.wait_ge(small_zero, 2)
                    for s0, w0, nn in ((0, LR_COL, RANK), (32, IF_COL, HC), (64, IF_COL + HC, HC)):
                        sp.dma_start(small_raw[:, :, s0:s0 + nn],
                                     I["w_in"][bass.ds(l, 1), :, w0:w0 + nn].rearrange("a (c p) n -> p (a c) n", p=P)
                                     ).then_inc(small_arrived, 16)

                def load_out(q):
                    load(B_OUT + q, B_OUT + q, four, rows(I["w_out"], 4 * (q % 2), 4 * (q % 2) + 4, (q // 2) * P))

                for q in range(LEAD + RAW):
                    load_out(q)
                def load_c(h):
                    sp.dma_start(s_cs[h % 2][:], I["state_mlstm_C"][bass.ds(l, 1), :, h].rearrange("a b k v -> k (a b) v")
                                 ).then_inc(sc_arrived[h % 2], 16)

                for ct in range(NCT):
                    sp.wait_ge(round_read, (ct + 1) * LIN)
                    if ct == 0:
                        sp.dma_start(O["gla_p"][bass.ds(l, 1)].rearrange("a b h k v -> (a b h k) v"),
                                     lin_st[:, 0, NCH - 1, :]).then_inc(state_stored, 16)
                        sp.dma_start(O["gla_s"][bass.ds(l, 1)].rearrange("a b h k v -> (h k) (a b) v"),
                                     s_lin[:, 0]).then_inc(state_stored, 16)
                    else:
                        h2 = slice(2 * ct - 2, 2 * ct)
                        sp.dma_start(O["hgrn_p"][bass.ds(l, 1), :, h2].rearrange("a b h k v -> (a b h k) v"),
                                     lin_st[:, ct, NCH - 1, :]).then_inc(state_stored, 16)
                        sp.dma_start(O["hgrn_s"][bass.ds(l, 1), :, h2].rearrange("a b h k v -> (h k) (a b) v"),
                                     s_lin[:, ct]).then_inc(state_stored, 16)
                    if ct == 0:
                        load_c(0)
                load_c(1)
                for h in range(HC):
                    sp.wait_ge(round_read, place("own", h) + 1)
                    sp.dma_start(O["c_p"][bass.ds(l, 1), 0, h].rearrange("a k v -> (a k) v"),
                                 c_st[:, NCH - 1, :]).then_inc(cp_stored, 16)
                    sp.wait_ge(round_read, place("samples", h) + 1)
                    sp.dma_start(O["c_s"][bass.ds(l, 1), :, h].rearrange("a b k v -> k (a b) v"), s_cs[h % 2][:]
                                 ).then_inc(cs_stored, 16)
                    if h + 2 < HC:
                        sp.wait_ge(cs_stored, 16 * (h + 1))
                        load_c(h + 2)
                sp.wait_ge(n_out_kept, 1)
                sp.dma_start(O["n_s"][bass.ds(l, 1)].rearrange("a b h k -> (a b h) k"), nrow[0:NS, :]).then_inc(state_stored, 16)
                sp.dma_start(O["n_p"][bass.ds(l, 1)].rearrange("a b h k -> (a b h) k"), nrow[NS:NS + HC, :]).then_inc(state_stored, 16)
                sp.dma_start(O["m_s"][bass.ds(l, 1)].rearrange("a b h -> h (a b)"), m_new[:],
                             allow_slow_non_contiguous=True).then_inc(state_stored, 16)
                sp.dma_start(O["m_p"][bass.ds(l, 1)].rearrange("a b h -> h (a b)"), m_ch[:, NCH:NCH + 1],
                             allow_slow_non_contiguous=True).then_inc(state_stored, 16)

                for q in range(LEAD + RAW, 2 * DC):
                    load_out(q)
                load_up(B_UP2, I["ffn2_w_gate"], I["ffn2_w_up"])
                load_down(B_DN2, I["ffn2_w_down"])
                sp.wait_ge(state_stored, 16 * 10)
                sp.wait_ge(cp_stored, 16 * HC)
                sp.wait_ge(cs_stored, 16 * HC)

            @block.gpsimd
            def _(pool):
                pool.sem_inc(w_split, RAW)

                def split(n, q, size):
                    m = size * P
                    pool.wait_ge(w_hi_ready, n + 1)
                    pool.tensor_tensor(w_lo[:, q % RING, 0:m], w_raw[:, q % RAW, 0:m],
                                       w_hi[:, q % RING, 0:m].bitcast(F32), ALU.subtract).then_inc(w_split, 1)

                def split_tiles(base, total, body, blocks, size, last=False):
                    def emit(t, j, i):
                        count = blocks - LEAD if last and isinstance(t, int) and t == total - 1 else blocks
                        for b in range(count):
                            split(base + t * blocks + b + LEAD, base + j * blocks + b + LEAD, size(j * blocks + b + LEAD))
                    tiles(pool, total, body, emit, peel=body if last else 0)

                def update_x(sub, y, every=1):
                    for c in range(0, DC, every):
                        pool.wait_ge(y_scaled, DC * sub + c + 1)
                        pool.tensor_tensor(x[:, c, :], x[:, c, :], y[:, c, :], ALU.add).then_inc(x_updated, 1)

                for q in range(LEAD):
                    split(q, q, 4)
                split_tiles(B_UP1, FC, 3, 4, four)
                split_tiles(B_DN1, DC, 2, DOWN_BLOCKS, down_size)
                update_x(0, y_ffn)
                split_tiles(B_IN, 3, 3, 2, four)
                pool.wait_ge(w_used, B_IN + RING)
                pool.memset(small_raw[:], 0.0).then_inc(small_zero, 1)
                pool.memset(qk_l[:], 0.0).then_inc(small_zero, 1)
                split_tiles(B_IN + 6, GATED - 3, 3, 2, four)
                pool.wait_ge(small_hi_ready, 1)
                pool.tensor_tensor(small_lo[:], small_raw[:], small_hi[:].bitcast(F32), ALU.subtract).then_inc(small_split, 1)
                split_tiles(B_IN + 2 * GATED, NPROJ - GATED, 3, 2, four)
                for i, ((hi, lo), row) in enumerate(zip(ROW_PARTS, SPREAD_ROWS)):
                    pool.wait_ge(rows_high, 4)
                    pool.tensor_tensor(lo[:], row[:], hi[:].bitcast(F32), ALU.subtract).then_inc(rows_split, 1)
                vi = 0
                for ct in range(NCT):
                    pool.wait_ge(round_read, ct * LIN + len(SCORE) + 1)
                    for hh, _, vt, c0 in heads(ct):
                        if vi >= 2:
                            pool.wait_ge(vexp_used, vi - 1)
                        half = v_exp[:, 512 * (vi % 2):512 * (vi % 2) + 512]
                        pool.tensor_tensor(half.rearrange("p (b v) -> p b v", v=DVA),
                                           v_tok_s[:, vt, c0:c0 + DVA].unsqueeze(1).broadcast_to([NS, NB, DVA]),
                                           bmask[:].unsqueeze(2).broadcast_to([NS, NB, DVA]), ALU.mult).then_inc(vexp_ready, 1)
                        vi += 1
                def gated(j):
                    o = proj[:, O_TILES[j], :]
                    pool.wait_ge(o_squared, j + 1)
                    pool.tensor_tensor(o, o, proj[:, GATE_TILES[j], :], ALU.mult).then_inc(o_gated, 1)

                for j in range(4):
                    gated(j)
                for h in range(HC):
                    pool.wait_ge(tok_ready, h + 1)
                    pool.wait_ge(vexp_used, vi)
                    pool.tensor_tensor(v_exp[:].rearrange("p (b v) -> p b v", v=DVC),
                                       v_tok_s[:, h % 2, :].unsqueeze(1).broadcast_to([NS, NB, DVC]),
                                       bmask[:].unsqueeze(2).broadcast_to([NS, NB, DVC]), ALU.mult).then_inc(vexp_ready, 1)
                    vi += 1
                for j in range(4, DC):
                    gated(j)
                split_tiles(B_OUT, DC, 3, 2, four)
                update_x(1, y_mix)
                split_tiles(B_UP2, FC, 3, 4, four)
                split_tiles(B_DN2, DC, 2, DOWN_BLOCKS, down_size, last=True)
                update_x(2, y_ffn, 2)

            @block.tensor
            def _(pe):
                pe.sem_inc(w_used, RING)

                def product(n, q, size, chunk0, chunks, dst, hi, lo, ready=None):
                    pe.wait_ge(w_split, n + 1 + RAW)
                    for c in range(size(q)):
                        k = chunk0 + c
                        if ready:
                            ready(k)
                        ws = slice(c * P, c * P + P)
                        for a, w, z in ((0, w_hi, hi), (1, w_hi, hi), (0, w_hi, lo), (1, w_hi, lo), (0, w_lo, hi), (1, w_lo, hi)):
                            mm = pe.matmul(dst[:, a, :], w[:, q % RING, ws], z[:, k, a * HT:a * HT + HT],
                                           start=(k == 0 and w is w_hi and z is hi),
                                           stop=(k == chunks - 1 and w is w_lo))
                    mm.then_inc(w_used, 1)

                def pre_sum(norm):
                    pe.wait_ge(x_summed, (DC - 1) * (norm + 1))
                    for a in range(2):
                        mm = pe.matmul(pair(3)[:, a, :], ones[:], acc[:, a * HT:a * HT + HT], start=True, stop=True)
                    mm.then_inc(xsq_done, 1)

                def post_sum(sub):
                    pe.wait_ge(y_summed, DC * (sub + 1) + 2)
                    for a in range(2):
                        mm = pe.matmul(pair(3)[:, a, :], ones[:], acc[:, a * HT:a * HT + HT], start=True, stop=True)
                    mm.then_inc(ssq_done, 1)

                def ffn(which, base_up, base_down, norm):
                    f0 = FC * which

                    def up(t, j, i):
                        for b in range(4):
                            p = (2 * j + b // 2) % 3
                            if b == 0:
                                pe.wait_ge(up_read, f0 + t + 1)
                            if b == 2:
                                pe.wait_ge(gate_scaled, f0 + t + 1)
                            first = isinstance(t, int) and t == 0 and b < 2
                            product(base_up + t * 4 + b, base_up + 4 * j + b, four, 4 * (b % 2), DC, pair(p), xn_hi, xn_lo,
                                    (lambda k: pe.wait_ge(xn_ready, DC * norm + k + 1)) if first else None)
                        if isinstance(t, int) and t == 0:
                            pre_sum(norm)

                    def down(t, j, i):
                        pe.wait_ge(y_copied, DC * 2 * which + t + 1)
                        for b in range(DOWN_BLOCKS):
                            product(base_down + t * DOWN_BLOCKS + b, base_down + DOWN_BLOCKS * j + b,
                                    lambda q: down_size(b), 4 * b, FC,
                                    pair(j), h_hi, h_lo, lambda k: pe.wait_ge(h_ready, f0 + k + 1 + 3))

                    tiles(pe, FC, 3, up, head=1)
                    pe.wait_ge(up_read, f0 + FC + 2)
                    pe.wait_ge(gate_scaled, f0 + FC + 1)
                    tiles(pe, DC, 2, down)

                ffn(0, B_UP1, B_DN1, 0)
                pe.wait_ge(n_arrived, 16)
                pe.transpose(ps[:, 5, 0:NS], nrow[0:NS, :], ident[0:NS, 0:NS]).then_inc(n_turned, 1)
                post_sum(0)
                pe.wait_ge(n_kept, 1)
                pe.wait_ge(std_done, 2)

                def proj_tile(t, j, i):
                    pe.wait_ge(proj_read, t + 1)
                    for b in range(2):
                        first = isinstance(t, int) and t == 0
                        product(B_IN + 2 * t + b, B_IN + 2 * j + b, four, 4 * b, DC, pair(j), xn_hi, xn_lo,
                                (lambda k: pe.wait_ge(xn_ready, DC + k + 1)) if first else None)
                    if isinstance(t, int) and t == 1:
                        pre_sum(1)
                tiles(pe, GATED, 3, proj_tile, head=1)
                pe.wait_ge(small_split, 1)
                pe.wait_ge(std_done, 3)
                for k in range(DC):
                    for a in range(2):
                        for w, z in ((small_hi, xn_hi), (small_hi, xn_lo), (small_lo, xn_hi)):
                            mm = pe.matmul(pair(3)[0:68, a, :], w[:, k, :], z[:, k, a * HT:a * HT + HT],
                                           start=(k == 0 and w is small_hi and z is xn_hi),
                                           stop=(k == DC - 1 and w is small_lo))
                mm.then_inc(small_done, 1)

                def proj_tile2(t, j, i):
                    proj_tile(GATED + t, j, None)
                    if isinstance(t, int) and t == 0:
                        pe.wait_ge(rows_read, 1)
                        pe.wait_ge(row_step, 2)
                        for a in range(2):
                            mm = pe.matmul(pair(3)[:, a, :], wlr[:], q_st[0:RANK, a * HT:a * HT + HT], start=True, stop=True)
                        mm.then_inc(lowrank_done, 1)
                    if isinstance(t, int) and t == 8:
                        pe.wait_ge(row_step, ROW_STEPS)
                        for r, row in enumerate((row_g, row_w)):
                            for c in range(NCH + 1):
                                w = P if c < NCH else NS
                                mm = pe.transpose(ps[0:w, 6, 64 * r + c * HC:64 * r + c * HC + HC], row[:, c * P:c * P + w],
                                                  ident[0:HC, 0:HC])
                        mm.then_inc(cols_turned, 1)
                tiles(pe, NPROJ - GATED, 3, proj_tile2, head=3)
                pe.wait_ge(u_ready, 2)
                pe.wait_ge(proj_read, NPROJ + 3)

                def begin(k):
                    if k == 1:
                        pe.wait_ge(cols_kept, 3)
                    if k >= 2:
                        pe.wait_ge(round_read, k - 1)
                    return 4 * (k % 2)

                for ct in range(NCT):
                    for i, (kind, r) in enumerate(SCORE):
                        b0 = begin(ct * LIN + i)
                        q, k = proj[:, q_tile(ct), :], proj[:, k_tile(ct), :]
                        if kind == "diag":
                            pe.wait_ge(qk_ready, ct + 1)
                            for c in range(NCH):
                                for hh, rows_, _, _ in heads(ct):
                                    mm = pe.matmul(ps[:, b0 + hh, c:c + 1], q_st[rows_, c * P:c * P + P], ones[rows_, 0:1],
                                                   start=True, stop=True)
                            mm.then_inc(round_done, 1)
                            continue
                        if kind == "level":
                            g = ct * NL + r
                            pe.wait_ge(scaled, g + 1)
                            q, k = qk_l[:, g % 2, 0, :], qk_l[:, g % 2, 1, :]
                        if kind == "samples":
                            for hh, rows_, _, _ in heads(ct):
                                pairs = [(q, k)] + [(qk_l[:, (ct * NL + m) % 2, 0, :], qk_l[:, (ct * NL + m) % 2, 1, :])
                                                    for m in SAMPLE_LEVELS]
                                for n, (qs, ks) in enumerate(pairs):
                                    mm = pe.matmul(ps[0:NS, b0 + hh, n * NS:n * NS + NS], ks[rows_, SEQ:T], qs[rows_, SEQ:T],
                                                   start=True, stop=True)
                        else:
                            for c in range(NCH):
                                cs = slice(c * P, c * P + P)
                                for hh, rows_, _, _ in heads(ct):
                                    mm = pe.matmul(ps[:, b0 + hh, cs], k[rows_, cs], q[rows_, cs], start=True, stop=True)
                        mm.then_inc(round_done, 1)
                    k0 = ct * LIN + len(SCORE)
                    b0 = begin(k0)
                    pe.wait_ge(st_scaled, ct + 1)
                    srcs = [k_st[:, :]] + [proj[:, v, :] for v in v_tiles(ct)]
                    for n, src in enumerate(srcs):
                        for c in range(NCH):
                            pe.transpose(ps[:, b0 + (0, 2, 3)[n], c * P:c * P + P], src[:, c * P:c * P + P], ident[:])
                        mm = pe.transpose(ps[0:NS, b0 + 1, n * P:n * P + P], src[:, SEQ:T], ident[:])
                    mm.then_inc(round_done, 1)
                    b0 = begin(k0 + 1)
                    pe.wait_ge(round_read, k0 + 1)
                    for hh, rows_, vt, c0 in heads(ct):
                        for c in range(NCH):
                            mm = pe.matmul(ps[rows_, b0, c * 64:c * 64 + 64], k_tok[:, c * P + rows_.start:c * P + rows_.stop],
                                           v_tok[:, vt, c * P + c0:c * P + c0 + 64], start=True, stop=True)
                    mm.then_inc(round_done, 1)
                    b0 = begin(k0 + 2)
                    pe.wait_ge(round_read, k0 + 2)
                    for hh, rows_, vt, c0 in heads(ct):
                        for c in range(NCH):
                            cs = slice(c * P, c * P + P)
                            dst = ps[c0:c0 + 64, b0 + hh, cs]
                            mm = pe.matmul(dst, v_tok[:, vt, c * P + c0:c * P + c0 + 64], scores[:, hh, cs],
                                           start=True, stop=(c == 0))
                            if c:
                                mm = pe.matmul(dst, lin_st[rows_, ct, c - 1, :], q_st[rows_, cs], start=False, stop=True)
                    mm.then_inc(round_done, 1)
                    b0 = begin(k0 + 3)
                    pe.wait_ge(slin_arrived, 48)
                    for hh, rows_, vt, c0 in heads(ct):
                        pe.matmul(ps[c0:c0 + 64, b0, 64 + NS * hh:64 + NS * hh + NS], v_tok_s[:, vt, c0:c0 + 64],
                                  scores_s[:, hh, :], start=True, stop=True)
                    for b in range(NB):
                        for hh, rows_, vt, c0 in heads(ct):
                            mm = pe.matmul(ps[c0:c0 + 64, b0 + hh, b * DS:b * DS + DS], s_lin[rows_, ct, b, :],
                                           q_st[rows_, SEQ + b * DS:SEQ + b * DS + DS], start=True, stop=True)
                    mm.then_inc(round_done, 1)
                    b0 = begin(k0 + 4)
                    for hh, rows_, vt, c0 in heads(ct):
                        vi = (0, 4, 6)[ct] + hh
                        pe.wait_ge(vexp_ready, vi + 1)
                        pe.matmul(ps[rows_, b0, :], k_tok_s[:, 0, rows_], v_exp[:, 512 * (vi % 2):512 * (vi % 2) + 512],
                                  start=True, stop=True).then_inc(vexp_used, 1)
                    pe.wait_ge(vexp_used, (4, 6, 8)[ct])
                    pe.sem_inc(round_done, 1)

                pe.wait_ge(rows_split, 3)

                def spread(h, b0):
                    for n, parts in enumerate(ROW_PARTS):
                        for i, row in enumerate(parts):
                            pe.matmul(ps[:, b0 + n, 0:SEQ], sel_r[:, h, :], row[:, 0:SEQ], start=(i == 0), stop=(i == 1))
                        for i, row in enumerate(parts):
                            mm = pe.matmul(ps[:, b0 + 3, n * NS:n * NS + NS], sel_r[:, h, :], row[:, SEQ:T],
                                           start=(i == 0), stop=(i == 1))
                    mm.then_inc(round_done, 1)

                def qk(h, b0):
                    q, k, v = proj[:, CQ + h, :], proj[:, CK + h, :], proj[:, CV + h, :]
                    for c in range(NCH):
                        cs = slice(c * P, c * P + P)
                        pe.matmul(ps[:, b0, cs], k[:, cs], q[:, cs], start=True, stop=True)
                        pe.transpose(ps[:, b0 + 2, cs], k[:, cs], ident[:])
                        pe.transpose(ps[:, b0 + 3, cs], v[:, cs], ident[:])
                    pe.matmul(ps[0:NS, b0 + 1, 0:NS], k[:, SEQ:T], q[:, SEQ:T], start=True, stop=True)
                    pe.transpose(ps[0:NS, b0 + 1, 64:64 + P], k[:, SEQ:T], ident[:])
                    pe.transpose(ps[0:NS, b0 + 1, 192:192 + P], v[:, SEQ:T], ident[:]).then_inc(round_done, 1)

                def own(h, b0):
                    pe.wait_ge(round_read, place("qk", h) + 1)
                    for c in range(NCH):
                        cs = slice(c * P, c * P + P)
                        pe.matmul(ps[:, b0, cs], k_tok[:, cs], v_tok[:, 0, cs], start=True, stop=True)
                        mm = pe.matmul(ps[:, b0 + 1, c:c + 1], k_tok[:, cs], ones[:, 0:1], start=True, stop=True)
                    mm.then_inc(round_done, 1)

                def out(h, b0):
                    q, dmat, s_c = proj[:, CQ + h, :], dmats[h % 2], s_cs[h % 2]
                    pe.wait_ge(round_read, place("own", h) + 1)
                    for c in range(NCH):
                        cs = slice(c * P, c * P + P)
                        pe.matmul(ps[:, b0, cs], v_tok[:, 0, cs], pmat[:, 0, cs], start=True, stop=(c == 0))
                        if c:
                            pe.matmul(ps[:, b0, cs], c_st[:, c - 1, :], q[:, cs], start=False, stop=True)
                        pe.matmul(ps[:, b0 + 1, cs], ones[:], pmat[:, 0, cs], start=True, stop=(c == 0))
                        if c:
                            pe.matmul(ps[:, b0 + 1, cs], ones[:], dmat[:, cs], start=False, stop=True)
                    pe.matmul(ps[:, b0 + 2, 0:NS], v_tok_s[:, h % 2, :], scores_s[:, 0, :], start=True, stop=True)
                    pe.wait_ge(sc_arrived[h % 2], 16 * (h // 2 + 1))
                    for b in range(NB):
                        pe.matmul(ps[:, b0 + 2, 64 + b * DS:64 + b * DS + DS], s_c[:, b, :],
                                  q[:, SEQ + b * DS:SEQ + b * DS + DS], start=True, stop=True)
                    pe.matmul(ps[:, b0 + 3, 0:NS], ones[0:NS, :], scores_s[:, 0, :], start=True, stop=False)
                    pe.matmul(ps[:, b0 + 3, 0:NS], ones[:], dmat[:, SEQ:T], start=False, stop=True).then_inc(round_done, 1)

                def samples(h, b0):
                    pe.wait_ge(vexp_ready, 8 + h + 1)
                    for a in range(2):
                        pe.matmul(ps[:, b0 + a, :], k_tok_s[:, h % 2, :], v_exp[:, a * 512:a * 512 + 512], start=True, stop=True)
                    pe.matmul(ps[:, b0 + 2, 0:NB], k_tok_s[:, h % 2, :], bmask[:], start=True, stop=True).then_inc(vexp_used, 1)
                    pe.wait_ge(vexp_used, 8 + h + 1)
                    pe.sem_inc(round_done, 1)

                def norm(n, b0):
                    for j in (2 * n, 2 * n + 1):
                        pe.wait_ge(o_squared, j + 1)
                        for a in range(2):
                            mm = pe.matmul(ps[:, b0 + 2 * (j % 2) + a, 0:HT], blk[:] if j < 4 else ones[:],
                                           head_sq[:, j % 3, a * HT:a * HT + HT], start=True, stop=True)
                        mm.then_inc(o_ssq, 1)
                    pe.wait_ge(o_ssq, 2 * n + 2)
                    pe.sem_inc(round_done, 1)

                program_of = {"spread": spread, "qk": qk, "own": own, "out": out, "samples": samples, "norm": norm}
                for kind, n in SEQUENCE:
                    program_of[kind](n, begin(place(kind, n)))
                pe.wait_ge(round_read, NROUND)
                pe.transpose(ps[0:NS + HC, 7, 0:P], n_all[:], ident[:]).then_inc(n_out_turned, 1)

                pe.wait_ge(o_ln, DC)

                def out_tile(t, j, i):
                    pe.wait_ge(y_copied, DC + t + 1)
                    for b in range(2):
                        product(B_OUT + 2 * t + b, B_OUT + 2 * j + b, four, 4 * b, DC, pair(j), xn_hi, xn_lo,
                                lambda k: pe.wait_ge(m_ready, k + 1))
                tiles(pe, DC, 3, out_tile)
                pe.wait_ge(n_out_kept, 1)
                post_sum(1)
                pe.wait_ge(std_done, 4)
                ffn(1, B_UP2, B_DN2, 2)
                post_sum(2)

            @block.scalar
            def _(act):
                def high(n, q, div, size):
                    m = size * P
                    act.wait_ge(w_arrived[q % RAW], 16 * div)
                    act.wait_ge(w_used, n + 1)
                    act.activation(w_hi[:, q % RING, 0:m], w_raw[:, q % RAW, 0:m], ACT.Copy).then_inc(w_hi_ready, 1)

                def high_next(base, per_tile, body, t, j, i, places, size):
                    for b in places:
                        q = base + j * per_tile + b + LEAD
                        high(base + t * per_tile + b + LEAD, q, i * (body * per_tile // RAW) + q // RAW + 1,
                             size(j * per_tile + b + LEAD))

                def split_x(norm, between=None):
                    for c in range(DC):
                        if norm:
                            act.wait_ge(x_updated, DC * (norm - 1) + c + 1)
                        g = 2 * norm * DC + c
                        act.activation(xn_hi[:, c, :], x[:, c, :], ACT.Copy, scale=par[:, g:g + 1]).then_inc(xn_hi_ready, 1)
                        act.activation(x_sq[:, c, :], x[:, c, :], ACT.Square).then_inc(x_squared, 1)
                        if between:
                            between(c)

                def root(k):
                    if k % 2:
                        act.wait_ge(xsq_done, k // 2 + 1)
                    else:
                        act.wait_ge(ssq_done, k // 2)
                    act.activation(halves(std[:]), pair(3), ACT.Sqrt, bias=eps_t[:, 0:1], scale=1.0 / D).then_inc(std_done, 1)

                def ffn(which, base_up, base_down, last):
                    f0 = FC * which

                    def up(t, j, i):
                        if not (isinstance(t, int) and t == 0):
                            high_next(base_up, 4, 3, t, j, i, range(4), four)
                        act.wait_ge(gate_scaled, f0 + t + 1 + 1)
                        act.activation(gs[:, j, :], gs[:, j, :], ACT.Silu).then_inc(silu_done, 1)
                        act.wait_ge(h_scaled, f0 + t + 1)
                        act.activation(h_hi[:, bass.ds(t, 1), :].rearrange("p a n -> p (a n)"), gs[:, j, :], ACT.Copy
                                       ).then_inc(h_hi_ready, 1)

                    def down(t, j, i, ahead=True):
                        if ahead:
                            high_next(base_down, DOWN_BLOCKS, 2, t, j, i, range(DOWN_BLOCKS), down_size)
                        else:
                            high_next(base_down, DOWN_BLOCKS, 2, t, j, i, range(DOWN_BLOCKS - LEAD), down_size)
                        y_square(DC * 2 * which, base_down, DOWN_BLOCKS, t, j)

                    high_next(base_up, 4, 3, 0, 0, 0, range(4), four)
                    root(4 * which + 1)
                    tiles(act, FC, 3, up, head=1)
                    act.wait_ge(h_ready, f0 + FC + 3)
                    if last:
                        tiles(act, DC, 2, lambda t, j, i: down(t, j, i, not (isinstance(t, int) and t == DC - 1)), peel=2)
                    else:
                        tiles(act, DC, 2, down)

                def y_square(y0, base, blocks, t, j):
                    act.wait_ge(w_used, base + (t + 1) * blocks + RING)
                    act.wait_ge(y_summed, y0 + t + 1)
                    act.activation(halves(gs[:, j, :]), pair(j), ACT.Square).then_inc(y_squared, 1)

                act.wait_ge(par_kept, 1)
                split_x(0, lambda c: high(c, c, c // RAW + 1, 4) if c < LEAD else None)
                ffn(0, B_UP1, B_DN1, False)
                root(2)
                split_x(1)
                high_next(B_IN, 2, 3, 0, 0, 0, (0, 1), four)
                high_next(B_IN, 2, 3, 1, 1, 0, (0, 1), four)
                root(3)
                tiles(act, GATED, 3, lambda t, j, i: high_next(
                    B_IN, 2, 3, t, j, i, () if isinstance(t, int) and t < 2 else (0, 1), four), head=1)
                act.wait_ge(small_arrived, 16 * 6)
                act.activation(small_hi[:], small_raw[:], ACT.Copy).then_inc(small_hi_ready, 1)

                def silus(tiles_):
                    act.wait_ge(proj_read, CQ + 3)
                    for t in tiles_:
                        act.activation(proj[:, t, :], proj[:, t, :], ACT.Silu).then_inc(gates_done, 1)

                def log_sigmoid(step):
                    u, row = ex_l[:, 0, :], row_a[:]
                    if step == 0:
                        act.wait_ge(u_ready, 2)
                        act.activation(u, e_st[:], ACT.Abs).then_inc(lsig_step, 1)
                        act.activation(row, row_f[:], ACT.Abs).then_inc(lsig_step, 1)
                    elif step == 1:
                        act.wait_ge(lsig_step, 2)
                        act.activation(u, u, ACT.Exp, scale=-1.0).then_inc(lsig_step, 1)
                        act.activation(row, row, ACT.Exp, scale=-1.0).then_inc(lsig_step, 1)
                    else:
                        act.wait_ge(lsig_step, 4)
                        act.activation(u, u, ACT.Ln, bias=1.0).then_inc(lsig_step, 1)
                        act.activation(row, row, ACT.Ln, bias=1.0).then_inc(lsig_step, 1)

                def proj_gates(t, j, i):
                    high_next(B_IN + 2 * GATED, 2, 3, t, j, i, (0, 1), four)
                    if isinstance(t, int):
                        if t == 0:
                            silus((AG, AG + 1, BG))
                        elif t == 1:
                            silus((BG + 1, BQ, BQ + 1))
                        elif t == 2:
                            for f in (BF, BF + 1):
                                act.activation(proj[:, f, :], proj[:, f, :], ACT.Sigmoid, scale=-1.0).then_inc(gates_done, 1)
                            log_sigmoid(0)
                        elif t == 3:
                            log_sigmoid(1)
                            log_sigmoid(2)
                        elif t == 4:
                            act.wait_ge(kb_ready, 3)
                            for f in range(2):
                                act.activation(qk_l[:, f, 0, :], proj[:, BF + f, :], ACT.Ln, bias=1.0, scale=-1.0
                                               ).then_inc(logf_ready, 1)
                tiles(act, NPROJ - GATED, 3, proj_gates, head=2)
                act.wait_ge(cols_turned, 1)
                act.activation(wcol[:, 0:NCH * HC], ps[:, 6, 64:64 + NCH * HC], ACT.Exp).then_inc(cols_kept, 1)
                act.activation(wcol[0:NS, NCH * HC:], ps[0:NS, 6, 64 + NCH * HC:64 + (NCH + 1) * HC], ACT.Exp).then_inc(cols_kept, 1)
                act.wait_ge(proj_read, NPROJ + 3)

                for (hi, _), row in zip(ROW_PARTS, SPREAD_ROWS):
                    act.activation(hi[:], row[:], ACT.Copy).then_inc(rows_high, 1)
                act.activation(sel_r[:], sel[:], ACT.Copy).then_inc(rows_high, 1)

                for ct in range(NCT):
                    if ct == 1:
                        for t in (CO, CO + 1, CO + 2, CO + 3):
                            act.activation(proj[:, t, :], proj[:, t, :], ACT.Sigmoid).then_inc(gates_done, 1)
                    sc = 1.0 / TAU if ct == 0 else 1.0
                    for r, h in enumerate(LEVELS):
                        g = ct * NL + r
                        end = T if 2 * h <= DS else SEQ
                        act.wait_ge(expo_arg, g + 1)
                        act.activation(ex_l[:, g % 2, 0:end], ex_l[:, g % 2, 0:end], ACT.Exp, scale=sc).then_inc(expo_val, 1)
                        if r == 1:
                            act.wait_ge(st_arg, ct + 1)
                            act.activation(e_st[:], bcum[:, ct, :], ACT.Exp, scale=sc)
                            act.activation(k_st[:], k_st[:], ACT.Exp, scale=sc).then_inc(st_val, 1)

                def weights(h):
                    k0 = place("spread", h)
                    b0 = 4 * (k0 % 2)
                    dmat, wprev, enm = dmats[h % 2], wprevs[h % 2], enms[h % 2]
                    act.wait_ge(round_done, k0 + 1)
                    if h >= 2:
                        act.wait_ge(o_squared, 4 + h - 2 + 1)
                    else:
                        act.wait_ge(round_read, NCT * LIN)
                    act.activation(wprev[:, 0:SEQ], ps[:, b0 + 1, 0:SEQ], ACT.Exp)
                    act.activation(wprev[:, SEQ:T], ps[:, b0 + 3, NS:2 * NS], ACT.Exp)
                    act.activation(enm[:, 0:SEQ], ps[:, b0 + 2, 0:SEQ], ACT.Exp, scale=-1.0)
                    act.activation(enm[:, SEQ:T], ps[:, b0 + 3, 2 * NS:3 * NS], ACT.Exp, scale=-1.0).then_inc(c_val, 1)
                    act.wait_ge(round_read, k0 + 1)
                    act.wait_ge(wcol_ready, 1)
                    for c in range(NCH):
                        cs = slice(c * P, c * P + P)
                        act.activation(dmat[:, cs], dmat[:, cs], ACT.Exp, bias=gcol[:, c * HC + h:c * HC + h + 1])
                    act.activation(dmat[0:NS, SEQ:T], dmat[0:NS, SEQ:T], ACT.Exp,
                                   bias=gcol[0:NS, NCH * HC + h:NCH * HC + h + 1]).then_inc(d_ready, 1)

                def tokens(h):
                    k0 = place("qk", h)
                    b0 = 4 * (k0 % 2)
                    act.wait_ge(round_done, k0 + 1)
                    for c in range(NCH):
                        cs = slice(c * P, c * P + P)
                        act.activation(k_tok[:, cs], ps[:, b0 + 2, cs], ACT.Copy, scale=wcol[:, c * HC + h:c * HC + h + 1])
                    act.activation(k_tok_s[:, h % 2, :], ps[0:NS, b0 + 1, 64:64 + P], ACT.Copy,
                                   scale=wcol[0:NS, NCH * HC + h:NCH * HC + h + 1])
                    act.activation(v_tok[:, 0, :], ps[:, b0 + 3, :], ACT.Copy)
                    act.activation(v_tok_s[:, h % 2, :], ps[0:NS, b0 + 1, 192:192 + P], ACT.Copy).then_inc(tok_ready, 1)

                def denominator(h):
                    k0 = place("out", h)
                    b0 = 4 * (k0 % 2)
                    act.wait_ge(round_done, k0 + 1)
                    act.activation(dmats[h % 2][:, 0:SEQ], ps[:, b0 + 1, :], ACT.Abs)
                    act.activation(dmats[h % 2][:, SEQ:T], ps[:, b0 + 3, 0:NS], ACT.Abs)
                    act.activation(proj[:, CV + h, 0:SEQ], ps[:, b0, :], ACT.Copy).then_inc(den_abs, 1)

                def head_logs(n):
                    b0 = 4 * (place("norm", n) % 2)
                    for j in (2 * n, 2 * n + 1):
                        act.wait_ge(o_ssq, j + 1)
                        if j >= 4:
                            act.wait_ge(o_norm, j - 3)
                        act.activation(halves(head_std[:, j % 4, :]), ps[:, b0 + 2 * (j % 2):b0 + 2 * (j % 2) + 2, 0:HT],
                                       ACT.Ln, bias=eps_t[:, 0:1], scale=1.0 / (DVA if j < 4 else DVC)).then_inc(o_ln, 1)

                def head_roots(j0):
                    for j in range(j0, j0 + 4):
                        act.wait_ge(o_ln, j + 1)
                        act.activation(head_std[:, j % 4, :], head_std[:, j % 4, :], ACT.Exp, scale=-0.5).then_inc(o_std, 1)

                def mixed_high(j):
                    act.wait_ge(o_norm, j + 1)
                    act.activation(xn_hi[:, j, :], proj[:, O_TILES[j], :], ACT.Copy).then_inc(m_hi_ready, 1)

                weights(0)
                head_logs(0)
                tokens(0)
                head_logs(1)
                head_roots(0)
                for h in range(HC):
                    if h:
                        tokens(h)
                    if h + 1 < HC:
                        weights(h + 1)
                    else:
                        head_logs(2)
                    denominator(h)
                act.wait_ge(round_done, place("samples", HC - 1) + 1)
                act.wait_ge(cp_stored, 16 * HC)
                act.wait_ge(state_stored, 16 * 6)
                for j in range(4):
                    mixed_high(j)
                head_logs(3)
                head_roots(4)
                for j in range(4, DC):
                    mixed_high(j)
                act.wait_ge(cs_stored, 16 * HC)

                def out_tile(t, j, i):
                    high_next(B_OUT, 2, 3, t, j, i, (0, 1), four)
                    y_square(DC, B_OUT, 2, t, j)
                tiles(act, DC, 3, out_tile)
                root(4)
                split_x(2)
                ffn(1, B_UP2, B_DN2, True)
                root(6)

            @block.vector
            def _(dve):
                dve.sem_inc(gate_scaled, 1)
                dve.sem_inc(up_read, 2)
                dve.sem_inc(h_ready, 3)
                dve.sem_inc(y_copied, 2)
                dve.sem_inc(y_summed, 2)
                dve.sem_inc(proj_read, 3)

                def gain(g, c):
                    return par[:, g * DC + c:g * DC + c + 1]

                def low_x(norm, c):
                    dve.wait_ge(xn_hi_ready, DC * norm + c + 1)
                    dve.scalar_tensor_tensor(xn_lo[:, c, :], x[:, c, :], gain(2 * norm, c), xn_hi[:, c, :].bitcast(F32),
                                             ALU.mult, ALU.subtract).then_inc(xn_ready, 1)

                def scale_y(sub, y, lag=2):
                    for c in range(DC + lag):
                        if c < DC:
                            dve.scalar_tensor_tensor(y[:, c, :], y[:, c, :], gain(2 * sub + 1, c), rstd[:],
                                                     ALU.mult, ALU.mult).then_inc(y_scaled, 1)
                        if c >= lag:
                            low_x(sub + 1, c - lag)

                def sum_x(norm):
                    n0 = (DC - 1) * norm
                    for c in range(1, DC):
                        dve.wait_ge(x_squared, DC * norm + c + 1)
                        if c > 1:
                            dve.wait_ge(x_summed, n0 + c - 1)
                        dve.tensor_tensor(acc[:], x_sq[:, 0, :] if c == 1 else acc[:], x_sq[:, c, :], ALU.add).then_inc(x_summed, 1)

                def rms_inverse(k):
                    dve.wait_ge(std_done, k)
                    dve.reciprocal(rstd[:], std[:]).then_inc(rstd_done, 1)
                    dve.wait_ge(rstd_done, k)

                def keep_y(y0, y):
                    def emit(t, j, i):
                        dve.wait_ge(y_squared, y0 + t + 1)
                        dve.wait_ge(y_summed, y0 + t + 2)
                        dve.tensor_tensor(acc[:], acc[:], gs[:, j, :], ALU.add).then_inc(y_summed, 1)
                        dve.tensor_copy(y[:, bass.ds(t, 1), :].rearrange("p o (a n) -> p (o a) n", a=2), pair(j)
                                        ).then_inc(y_copied, 1)
                    return emit

                def clear_acc(n):
                    dve.memset(acc[:], 0.0).then_inc(acc_zero, 1)
                    dve.wait_ge(acc_zero, n)

                def ffn(which, base_up, base_down):
                    f0 = FC * which

                    def up(t, j, i):
                        g = gs[:, j, :]
                        dve.wait_ge(w_used, base_up + 4 * t + 2 + RING)
                        dve.wait_ge(h_ready, f0 + t + 1)
                        dve.tensor_tensor(halves(g), pair((2 * j) % 3), halves(rstd[:]), ALU.mult).then_inc(gate_scaled, 1)
                        dve.wait_ge(silu_done, f0 + t + 1)
                        dve.wait_ge(w_used, base_up + 4 * t + 4 + RING)
                        dve.tensor_tensor(halves(g), halves(g), pair((2 * j + 1) % 3), ALU.mult).then_inc(up_read, 1)
                        dve.wait_ge(up_read, f0 + t + 1 + 2)
                        dve.tensor_tensor(g, g, rstd[:], ALU.mult).then_inc(h_scaled, 1)
                        dve.wait_ge(h_hi_ready, f0 + t + 1)
                        dve.tensor_tensor(h_lo[:, bass.ds(t, 1), :].rearrange("p a n -> p (a n)"), g,
                                          h_hi[:, bass.ds(t, 1), :].rearrange("p a n -> p (a n)").bitcast(F32), ALU.subtract
                                          ).then_inc(h_ready, 1)
                    rms_inverse(4 * which + 1)
                    tiles(dve, FC, 3, up)
                    clear_acc(2 * which + 1)
                    tiles(dve, DC, 2, keep_y(DC * 2 * which, y_ffn))

                dve.tensor_copy(par[:].unsqueeze(1), par_all[:, bass.ds(l, 1), :]).then_inc(par_kept, 1)
                dve.wait_ge(par_kept, 1)
                for c in range(DC):
                    low_x(0, c)
                sum_x(0)
                ffn(0, B_UP1, B_DN1)
                dve.wait_ge(n_turned, 1)
                dve.tensor_copy(n_s[:], ps[:, 5, 0:NS]).then_inc(n_kept, 1)
                rms_inverse(2)
                scale_y(0, y_ffn)
                sum_x(1)
                rms_inverse(3)

                def proj_tile(t, j, i):
                    dve.wait_ge(w_used, B_IN + 2 * t + 2 + RING)
                    dve.tensor_tensor(proj[:, bass.ds(t, 1), :].rearrange("p o (a n) -> p (o a) n", a=2), pair(j),
                                      halves(rstd[:]), ALU.mult).then_inc(proj_read, 1)
                tiles(dve, GATED, 3, proj_tile)
                dve.wait_ge(small_done, 1)
                dve.tensor_tensor(halves(q_st[0:RANK, :]), pair(3)[0:RANK], halves(rstd[0:RANK, :]), ALU.mult).then_inc(rows_read, 1)
                n = [0]

                def step(ins):
                    n[0] += 1
                    ins.then_inc(row_step, 1)
                    dve.wait_ge(row_step, n[0])

                step(dve.tensor_tensor(halves(row_g[:]), pair(3)[32:32 + HC], halves(rstd[32:32 + HC, :]), ALU.mult))
                step(dve.tensor_tensor(halves(row_f[:]), pair(3)[64:64 + HC], halves(rstd[64:64 + HC, :]), ALU.mult))
                step(dve.tensor_scalar(row_g[:], row_g[:], bias_if[:, 0:1], None, ALU.add))
                dve.tensor_scalar(row_f[:], row_f[:], bias_if[:, 1:2], None, ALU.add).then_inc(u_ready, 1)

                def seqs(row, first=0, count=DS):
                    return row.rearrange("p (b n) -> p b n", n=DS)[:, :, first:first + count]

                def proj_tile2(t, j, i):
                    proj_tile(GATED + t, j, None)
                    if not isinstance(t, int):
                        return
                    if t == 0:
                        dve.wait_ge(lowrank_done, 1)
                        dve.tensor_scalar(halves(e_st[:]), pair(3), par[:, BLR_ROW:BLR_ROW + 1], None, ALU.add).then_inc(u_ready, 1)
                        dve.tensor_copy(omlb_l[:].unsqueeze(1), omlb[:, bass.ds(l, 1), :]).then_inc(omlb_ready, 1)
                        dve.tensor_scalar(proj[:, AQ, :], proj[:, AQ, :], float(DKA) ** -0.5, None, ALU.mult).then_inc(kb_ready, 1)
                    elif t == 2:
                        dve.wait_ge(omlb_ready, 1)
                        for j in range(2):
                            dve.wait_ge(gates_done, 7 + j)
                            dve.tensor_scalar(proj[:, BF + j, :], proj[:, BF + j, :], omlb_l[:, j:j + 1], None, ALU.mult
                                              ).then_inc(kb_ready, 1)
                    elif t == 4:
                        dve.wait_ge(lsig_step, 6)
                        step(dve.scalar_tensor_tensor(k_st[:], e_st[:], 0.0, ex_l[:, 0, :], ALU.min, ALU.subtract))
                        dve.tensor_tensor_scan(bcum[:, 0, :], reset[:], k_st[:], 0.0, ALU.mult, ALU.add).then_inc(cum_ready, 1)
                        step(dve.scalar_tensor_tensor(row_mt[:], row_f[:], 0.0, row_a[:], ALU.min, ALU.subtract))
                        step(dve.tensor_tensor_scan(row_f[:], reset[0:HC, :], row_mt[:], 0.0, ALU.mult, ALU.add))
                        step(dve.tensor_tensor(row_g[:], row_g[:], row_f[:], ALU.subtract))
                    elif t == 5:
                        step(dve.memset(m_ch[:, 0:1], NEG))
                        for c in range(NCH):
                            cs, last = slice(c * P, c * P + P), slice(c * P + P - 1, c * P + P)
                            step(dve.tensor_tensor_scan(row_m[:, cs], row_g[:, cs], row_g[:, cs], m_ch[:, c:c + 1], ALU.max, ALU.max))
                            step(dve.tensor_tensor(m_ch[:, c + 1:c + 2], row_f[:, last], row_m[:, last], ALU.add))
                            dve.tensor_scalar(row_a[:, cs], row_m[:, cs], -1.0, m_ch[:, c:c + 1], ALU.mult, ALU.add)

                    elif t == 6:
                        dve.wait_ge(ms_arrived, 16)
                        step(dve.tensor_copy(g_s[:], row_g[:, SEQ:T]))
                        step(dve.tensor_tensor(seqs(g_s[:], 0, 1), seqs(g_s[:], 0, 1), m_s[:].unsqueeze(2), ALU.max))
                        step(dve.tensor_tensor_scan(row_m[:, SEQ:T], neg_s[:], g_s[:], 0.0, ALU.add, ALU.max))
                        rf, rm, rg, ra, rw = (r[:, SEQ:T] for r in (row_f, row_m, row_g, row_a, row_w))
                        step(dve.tensor_tensor(m_new[:].unsqueeze(2), seqs(rf, DS - 1, 1), seqs(rm, DS - 1, 1), ALU.add))
                        step(dve.tensor_tensor(seqs(ra), m_s[:].unsqueeze(2).broadcast_to([HC, NB, DS]), seqs(rm), ALU.subtract))
                        step(dve.tensor_tensor(row_mt[:], row_f[:], row_m[:], ALU.add))
                        step(dve.tensor_tensor(seqs(rw), seqs(rg), seqs(rm, DS - 1, 1).broadcast_to([HC, NB, DS]), ALU.subtract))

                        def chunks(row):
                            return row[:, 0:SEQ].rearrange("p (c n) -> p c n", n=P)
                        step(dve.tensor_tensor(chunks(row_w), chunks(row_g),
                                               chunks(row_m)[:, :, P - 1:P].broadcast_to([HC, NCH, P]), ALU.subtract))
                        assert n[0] == ROW_STEPS
                    elif t == 7:
                        for j in range(2):
                            dve.wait_ge(logf_ready, j + 1)
                            dve.tensor_tensor_scan(bcum[:, 1 + j, :], reset[:], qk_l[:, j, 0, :], 0.0, ALU.mult, ALU.add
                                                   ).then_inc(cum_ready, 1)
                tiles(dve, NPROJ - GATED, 3, proj_tile2, head=3)
                dve.wait_ge(cols_kept, 2)
                dve.tensor_copy(gcol[:, 0:NCH * HC], ps[:, 6, 0:NCH * HC])
                dve.tensor_copy(gcol[0:NS, NCH * HC:], ps[0:NS, 6, NCH * HC:(NCH + 1) * HC]).then_inc(cols_kept, 1)
                dve.wait_ge(cols_kept, 3)
                dve.tensor_scalar(wcol[:, 0:NCH * HC], wcol[:, 0:NCH * HC], KS, None, ALU.mult)
                dve.tensor_scalar(wcol[0:NS, NCH * HC:], wcol[0:NS, NCH * HC:], KS, None, ALU.mult).then_inc(wcol_ready, 1)
                dve.wait_ge(cum_ready, 3)
                dve.wait_ge(kb_ready, 3)

                def exponents(g):
                    ct, h = g // NL, LEVELS[g % NL]
                    end = T if 2 * h <= DS else SEQ
                    nblk = end // (2 * h)
                    b = bcum[:, ct, 0:end].rearrange("p (n h) -> p n h", h=2 * h)
                    e = ex_l[:, g % 2, 0:end].rearrange("p (n h) -> p n h", h=2 * h)
                    mid = b[:, :, h - 1:h].broadcast_to([P, nblk, h])
                    if g >= 2:
                        dve.wait_ge(scaled, g - 1)
                    dve.tensor_tensor(e[:, :, h:2 * h], b[:, :, h:2 * h], mid, ALU.subtract)
                    dve.tensor_tensor(e[:, :, 0:h], mid, b[:, :, 0:h], ALU.subtract).then_inc(expo_arg, 1)

                def decayed(g):
                    ct, h = g // NL, LEVELS[g % NL]
                    end = T if 2 * h <= DS else SEQ
                    e, q, k, eq, ek = (a[:, 0:end].rearrange("p (n h) -> p n h", h=2 * h) for a in (
                        ex_l[:, g % 2, :], proj[:, q_tile(ct), :], proj[:, k_tile(ct), :],
                        qk_l[:, g % 2, 0, :], qk_l[:, g % 2, 1, :]))
                    dve.wait_ge(expo_val, g + 1)
                    dve.tensor_tensor(eq[:, :, h:2 * h], q[:, :, h:2 * h], e[:, :, h:2 * h], ALU.mult)
                    dve.tensor_tensor(ek[:, :, 0:h], k[:, :, 0:h], e[:, :, 0:h], ALU.mult).then_inc(scaled, 1)

                def choose(ct, i):
                    kind, r = SCORE[i]
                    k = ct * LIN + i
                    b0 = 4 * (k % 2)
                    if k:
                        dve.wait_ge(round_read, k)
                    dve.wait_ge(round_done, k + 1)
                    nh = len(heads(ct))
                    chunk = "p h (c n) -> p h c n"

                    def over(m):
                        return m.unsqueeze(1).unsqueeze(1).broadcast_to([P, nh, NCH, P])

                    def over_s(m):
                        return m.unsqueeze(1).broadcast_to([NS, nh, NS])
                    main = scores[:, 0:nh, :].rearrange(chunk, n=P)
                    prod = ps[:, b0:b0 + nh, :].rearrange(chunk, n=P)
                    small = scores_s[:, 0:nh, :]
                    if kind == "diag":
                        ins = dve.tensor_tensor(main, over(ident[:]), ps[:, b0:b0 + nh, 0:NCH].unsqueeze(3).broadcast_to(
                            [P, nh, NCH, P]), ALU.mult)
                    elif kind == "level":
                        ins = dve.copy_predicated(main, over(lmask[:, r, :]), prod)
                    else:
                        chain(cnt, dve.tensor_tensor(small, ps[0:NS, b0:b0 + nh, 0:NS], over_s(ident[0:NS, 0:NS]), ALU.mult))
                        for n, m in enumerate(SAMPLE_LEVELS):
                            ins = dve.copy_predicated(small, over_s(lmask[0:NS, m, 0:NS]),
                                                      ps[0:NS, b0:b0 + nh, NS * (n + 1):NS * (n + 2)])
                            if n + 1 < len(SAMPLE_LEVELS):
                                chain(cnt, ins)
                    ins.then_inc(round_read, 1)

                def chain(count, ins):
                    ins.then_inc(st_step, 1)
                    count[0] += 1
                    dve.wait_ge(st_step, count[0])

                cnt = [0]
                dve.wait_ge(gates_done, 6)
                for ct in range(NCT):
                    g0 = ct * NL
                    b = bcum[:, ct, :]
                    bp = b[:, 0:SEQ].rearrange("p (c n) -> p c n", n=P)
                    kp = k_st[:, 0:SEQ].rearrange("p (c n) -> p c n", n=P)
                    dve.tensor_tensor(q_st[:], proj[:, q_tile(ct), :], proj[:, k_tile(ct), :], ALU.mult).then_inc(qk_ready, 1)
                    dve.tensor_tensor(kp, bp[:, :, P - 1:P].broadcast_to([P, NCH, P]), bp, ALU.subtract)
                    dve.tensor_tensor(seqs(k_st[:, SEQ:T]), seqs(b[:, SEQ:T], DS - 1, 1).broadcast_to([P, NB, DS]),
                                      seqs(b[:, SEQ:T]), ALU.subtract).then_inc(st_arg, 1)
                    exponents(g0)
                    exponents(g0 + 1)
                    decayed(g0)
                    choose(ct, 0)
                    for r in range(NL):
                        if r + 1 < NL:
                            decayed(g0 + r + 1)
                        if r + 2 < NL:
                            exponents(g0 + r + 2)
                        if r == NL - 1:
                            dve.wait_ge(st_val, ct + 1)
                            dve.tensor_tensor(q_st[:], proj[:, q_tile(ct), :], e_st[:], ALU.mult)
                            dve.tensor_tensor(k_st[:], proj[:, k_tile(ct), :], k_st[:], ALU.mult).then_inc(st_scaled, 1)
                        choose(ct, 1 + r)
                    choose(ct, 1 + NL)
                    k0 = ct * LIN + len(SCORE)
                    b0 = 4 * (k0 % 2)
                    dve.wait_ge(round_done, k0 + 1)
                    dve.tensor_copy(k_tok[:], ps[:, b0, :])
                    dve.tensor_copy(k_tok_s[:, 0, :], ps[0:NS, b0 + 1, 0:P])
                    for m in range(len(v_tiles(ct))):
                        dve.tensor_copy(v_tok[:, m, :], ps[:, b0 + 2 + m, :])
                        ins = dve.tensor_copy(v_tok_s[:, m, :], ps[0:NS, b0 + 1, P + m * P:2 * P + m * P])
                    ins.then_inc(round_read, 1)
                    b0 = 4 * ((k0 + 1) % 2)
                    dve.wait_ge(round_done, k0 + 2)
                    for c in range(NCH):
                        own = ps[:, b0, c * 64:c * 64 + 64]
                        if c == 0:
                            chain(cnt, dve.tensor_copy(lin_st[:, ct, 0, :], own))
                        else:
                            chain(cnt, dve.scalar_tensor_tensor(lin_st[:, ct, c, :], lin_st[:, ct, c - 1, :],
                                                                e_st[:, c * P + P - 1:c * P + P], own, ALU.mult, ALU.add))
                    dve.sem_inc(round_read, 1)
                    b0 = 4 * ((k0 + 2) % 2)
                    dve.wait_ge(round_done, k0 + 3)
                    for hh, _, vt, c0 in heads(ct):
                        ins = dve.tensor_copy(proj[c0:c0 + 64, v_tiles(ct)[vt], 0:SEQ], ps[c0:c0 + 64, b0 + hh, :])
                    ins.then_inc(round_read, 1)
                    b0 = 4 * ((k0 + 3) % 2)
                    dve.wait_ge(round_done, k0 + 4)
                    for hh, _, vt, c0 in heads(ct):
                        ins = dve.tensor_copy(proj[c0:c0 + 64, v_tiles(ct)[vt], SEQ:T],
                                              ps[c0:c0 + 64, b0, 64 + NS * hh:64 + NS * hh + NS])
                    chain(cnt, ins)
                    for hh, _, vt, c0 in heads(ct):
                        o = proj[c0:c0 + 64, v_tiles(ct)[vt], SEQ:T]
                        ins = dve.tensor_tensor(o, o, ps[c0:c0 + 64, b0 + hh, 0:NS], ALU.add)
                    ins.then_inc(round_read, 1)
                    b0 = 4 * ((k0 + 4) % 2)
                    chain(cnt, dve.tensor_tensor(s_lin[:, ct], s_lin[:, ct],
                                                 seqs(e_st[:, SEQ:T], DS - 1, 1).broadcast_to([P, NB, DVA]), ALU.mult))
                    dve.wait_ge(round_done, k0 + 5)
                    dve.tensor_tensor(s_lin[:, ct], s_lin[:, ct], ps[:, b0, :].rearrange("p (b v) -> p b v", v=DVA),
                                      ALU.add).then_inc(round_read, 1)

                cn = [0]

                def cstep(ins):
                    ins.then_inc(c_step, 1)
                    cn[0] += 1
                    dve.wait_ge(c_step, cn[0])

                def mask(h):
                    b0 = 4 * (place("spread", h) % 2)
                    dmat = dmats[h % 2]
                    dve.wait_ge(c_val, h + 1)
                    dve.scalar_tensor_tensor(dmat[:, 0:SEQ].rearrange("p (c n) -> p c n", n=P),
                                             ps[:, b0, :].rearrange("p (c n) -> p c n", n=P), -1.0,
                                             causal[:].unsqueeze(1).broadcast_to([P, NCH, P]), ALU.mult, ALU.add)
                    cstep(dve.scalar_tensor_tensor(dmat[0:NS, SEQ:T], ps[0:NS, b0 + 3, 0:NS], -1.0, causal_s[:],
                                                   ALU.mult, ALU.add))
                    dve.sem_inc(round_read, 1)

                def weighted(h):
                    k0 = place("qk", h)
                    b0 = 4 * (k0 % 2)
                    q, dmat = proj[:, CQ + h, :], dmats[h % 2]
                    dve.wait_ge(round_done, k0 + 1)
                    dve.wait_ge(d_ready, h + 1)
                    dve.scalar_tensor_tensor(pmat[:, 0, :], ps[:, b0, :], KS, dmat[:, 0:SEQ], ALU.mult, ALU.mult)
                    dve.wait_ge(tok_ready, h + 1)
                    dve.scalar_tensor_tensor(scores_s[:, 0, :], ps[0:NS, b0 + 1, 0:NS], KS, dmat[0:NS, SEQ:T],
                                             ALU.mult, ALU.mult)
                    cstep(dve.tensor_tensor(q, q, wprevs[h % 2][:], ALU.mult))
                    dve.sem_inc(round_read, 1)

                def normaliser(h):
                    return n_s[:].rearrange("p (b h) -> p b h", h=HC)[:, :, h:h + 1]

                def carry(h):
                    k0 = place("own", h)
                    b0 = 4 * (k0 % 2)
                    q, dmat, wprev = proj[:, CQ + h, :], dmats[h % 2], wprevs[h % 2]
                    dve.wait_ge(round_done, k0 + 1)
                    if h:
                        dve.wait_ge(cp_stored, 16 * h)
                    for c in range(NCH):
                        own = ps[:, b0, c * P:c * P + P]
                        nown = ps[:, b0 + 1, c:c + 1]
                        wo = wprev[:, c * P + P - 1:c * P + P]
                        if c == 0:
                            dve.tensor_copy(c_st[:, 0, :], own)
                            cstep(dve.tensor_copy(n_ch[:, 0:1], nown))
                        else:
                            dve.tensor_scalar(dmat[:, c * P:c * P + P], q[:, c * P:c * P + P], n_ch[:, c - 1:c], None, ALU.mult)
                            dve.scalar_tensor_tensor(c_st[:, c, :], c_st[:, c - 1, :], wo, own, ALU.mult, ALU.add)
                            cstep(dve.scalar_tensor_tensor(n_ch[:, c:c + 1], n_ch[:, c - 1:c], wo, nown, ALU.mult, ALU.add))
                    dve.tensor_copy(n_all[:, NS + h:NS + h + 1], n_ch[:, NCH - 1:NCH])
                    cstep(dve.tensor_tensor(seqs(dmat[:, SEQ:T]), seqs(q[:, SEQ:T]),
                                            normaliser(h).broadcast_to([P, NB, DS]), ALU.mult))
                    dve.sem_inc(round_read, 1)

                def numerator(h):
                    b0 = 4 * (place("out", h) % 2)
                    os = proj[:, CV + h, SEQ:T]
                    dve.wait_ge(den_abs, h + 1)
                    cstep(dve.tensor_copy(os, ps[:, b0 + 2, 0:NS]))
                    cstep(dve.tensor_tensor(os, os, ps[:, b0 + 2, 64:64 + NS], ALU.add))
                    dve.sem_inc(round_read, 1)

                def quotient(h):
                    o, dmat = proj[:, CV + h, :], dmats[h % 2]
                    cstep(dve.tensor_tensor(dmat[:], dmat[:], enms[h % 2][:], ALU.max))
                    cstep(dve.reciprocal(dmat[:], dmat[:]))
                    cstep(dve.tensor_tensor(o, o, dmat[:], ALU.mult))

                def sample_states(h):
                    k0 = place("samples", h)
                    b0 = 4 * (k0 % 2)
                    s_c = s_cs[h % 2]
                    wo = seqs(wprevs[h % 2][:, SEQ:T], DS - 1, 1)
                    na = n_all[:, 0:NS].rearrange("p (b h) -> p b h", h=HC)[:, :, h:h + 1]
                    dve.tensor_tensor(s_c[:], s_c[:], wo.broadcast_to([P, NB, DVC]), ALU.mult)
                    cstep(dve.tensor_tensor(na, normaliser(h), wo, ALU.mult))
                    dve.wait_ge(round_done, k0 + 1)
                    for a in range(2):
                        half = s_c[:, a * NB // 2:(a + 1) * NB // 2, :]
                        dve.tensor_tensor(half, half, ps[:, b0 + a, :].rearrange("p (b v) -> p b v", v=DVC), ALU.add)
                    cstep(dve.tensor_tensor(na, na, ps[:, b0 + 2, 0:NB].unsqueeze(2), ALU.add))
                    dve.sem_inc(round_read, 1)

                def head_square(j):
                    o = proj[:, O_TILES[j], :]
                    if j >= 3:
                        dve.wait_ge(o_ssq, j - 2)
                    dve.tensor_tensor(head_sq[:, j % 3, :], o, o, ALU.mult).then_inc(o_squared, 1)

                def logs_read(n):
                    dve.wait_ge(o_ln, 2 * n + 2)
                    dve.sem_inc(round_read, 1)

                def head_norm(j):
                    o = proj[:, O_TILES[j], :]
                    g = GN_ROW + (0 if j < 2 else 1 if j < 4 else 2)
                    dve.wait_ge(o_std, j + 1)
                    dve.wait_ge(o_gated, j + 1)
                    dve.scalar_tensor_tensor(o, o, par[:, g:g + 1], head_std[:, j % 4, :], ALU.mult, ALU.mult).then_inc(o_norm, 1)

                def mixed_low(j):
                    dve.wait_ge(m_hi_ready, j + 1)
                    dve.tensor_tensor(xn_lo[:, j, :], proj[:, O_TILES[j], :], xn_hi[:, j, :].bitcast(F32), ALU.subtract
                                      ).then_inc(m_ready, 1)

                dve.wait_ge(round_read, NCT * LIN)
                for j in range(3):
                    head_square(j)
                mask(0)
                head_square(3)
                logs_read(0)
                weighted(0)
                logs_read(1)
                carry(0)
                mask(1)
                for j in range(4):
                    head_norm(j)
                for h in range(HC):
                    numerator(h)
                    if h + 1 < HC:
                        weighted(h + 1)
                        carry(h + 1)
                        sample_states(h)
                    quotient(h)
                    head_square(4 + h)
                    if h + 2 < HC:
                        mask(h + 2)
                    elif h + 1 < HC:
                        logs_read(2)
                sample_states(HC - 1)
                for j in range(4):
                    mixed_low(j)
                logs_read(3)
                dve.wait_ge(n_out_turned, 1)
                dve.tensor_copy(nrow[:], ps[0:NS + HC, 7, 0:P]).then_inc(n_out_kept, 1)
                for j in range(4, DC):
                    head_norm(j)
                    if j > 4:
                        mixed_low(j - 1)
                mixed_low(DC - 1)
                clear_acc(2)
                tiles(dve, DC, 3, keep_y(DC, y_mix))
                rms_inverse(4)
                scale_y(1, y_mix)
                sum_x(2)
                ffn(1, B_UP2, B_DN2)
                rms_inverse(6)
                for c in range(DC + 1):
                    if c < DC:
                        dve.scalar_tensor_tensor(y_ffn[:, c, :], y_ffn[:, c, :], gain(5, c), rstd[:],
                                                 ALU.mult, ALU.mult).then_inc(y_scaled, 1)
                    if c and c % 2 == 0:
                        dve.wait_ge(y_scaled, 2 * DC + c)
                        dve.tensor_tensor(x[:, c - 1, :], x[:, c - 1, :], y_ffn[:, c - 1, :], ALU.add).then_inc(x_updated, 1)

        with nc.Fori(0, DEPTH) as l:
            with nc.Block() as block:
                layer(l, block)
            nc.sync.sem_clear(range(loop_sems[0].num, loop_sems[-1].num + 1))
            nc.all_engine_barrier(sem_only=True)

        with nc.Block() as block:

            @block.tensor
            def _(pe):
                for j in range(NCH + 1):
                    w = P if j < NCH else NS
                    if j >= 4:
                        pe.wait_ge(out_kept, j - 3)
                    for c in range(DC):
                        mm = pe.transpose(ps[0:w, 2 * (j % 4) + c // 4, (c % 4) * P:(c % 4) * P + P],
                                          x[:, c, j * P:j * P + w], ident[:])
                    mm.then_inc(out_turned, 1)

            @block.vector
            def _(dve):
                for j in range(NCH + 1):
                    w = P if j < NCH else NS
                    dve.wait_ge(out_turned, j + 1)
                    dve.tensor_copy(tok_out[0:w, j, :].rearrange("p (a n) -> p a n", a=2),
                                    ps[0:w, 2 * (j % 4):2 * (j % 4) + 2, :]).then_inc(out_kept, 1)

            @block.sync
            def _(sp):
                for j in range(NCH + 1):
                    sp.wait_ge(out_kept, j + 1)
                    if j < NCH:
                        sp.dma_start(O["y_prompt"][0, j * P:j * P + P, :], tok_out[:, j, :]).then_inc(out_stored, 16)
                    else:
                        sp.dma_start(O["y_sample"].rearrange("b t d -> (b t) d"), tok_out[0:NS, j, :]).then_inc(out_stored, 16)
                sp.wait_ge(out_stored, 16 * (NCH + 1))


OUTPUTS = ["y_prompt", "y_sample", "gla_p", "hgrn_p", "c_p", "n_p", "m_p", "gla_s", "hgrn_s", "c_s", "n_s", "m_s"]


def kernel(**inputs):
    import concourse.bacc as bacc
    from concourse.bass_utils import run_bass_kernel_spmd

    nc = bacc.Bacc("TRN2", target_bir_lowering=False, num_devices=1)
    arrays = {name: np.ascontiguousarray(a) for name, a in inputs.items()}
    ins = {name: nc.dram_tensor("in_" + name, a.shape, F32, kind="ExternalInput").ap() for name, a in arrays.items()}
    state = {"gla": "state_gla", "hgrn": "state_hgrn", "c": "state_mlstm_C", "n": "state_mlstm_n", "m": "state_mlstm_m"}
    outs = {}
    for name in OUTPUTS:
        kind, group = name.rsplit("_", 1)
        if kind == "y":
            shape = arrays["x_" + group].shape
        else:
            shape = list(arrays[state[kind]].shape)
            if group == "p":
                shape[1] = arrays["x_prompt"].shape[0]
        outs[name] = nc.dram_tensor("out_" + name, tuple(shape), F32, kind="ExternalOutput").ap()
    program(nc, ins, outs)
    r = run_bass_kernel_spmd(nc, [{"in_" + name: a for name, a in arrays.items()}], core_ids=[0])
    return tuple(r.results[0]["out_" + name] for name in OUTPUTS)
```
